# Optimizing a Trainium2 kernel written in Bass

```python
import jax, jax.numpy as jnp
from jax import lax
import numpy as np

D_MODEL = 1024
BATCH = 1
SEQ = 1024
DEPTH = 1
DEC_BATCH = 1
DEC_SEQ = 64
PAST_LEN = 1024

CHUNK = 64
NORM_EPS = 1e-6
LOG_FLOOR = 1e-30
HG_HEADS = 4
HG_DK = 128
HG_DV = 128
HG_KW = HG_HEADS * HG_DK
HG_W = HG_HEADS * HG_DV
GLA_HEADS = 4
GLA_DK = 64
GLA_DV = 128
GLA_KW = GLA_HEADS * GLA_DK
GLA_W = GLA_HEADS * GLA_DV
GLA_GATE_RANK = 16
GLA_GATE_NORM = 16.0
IN_SPLITS = (HG_KW, HG_KW, HG_W, HG_W, GLA_KW, GLA_KW, GLA_W, GLA_W, GLA_GATE_RANK, D_MODEL, D_MODEL)
IN_COLS = sum(IN_SPLITS)
N_GROUPS = 4
EXPERTS_PER_GROUP = 8
N_EXPERTS = N_GROUPS * EXPERTS_PER_GROUP
TOPK_IN_GROUP = 2
D_EXPERT = 512
MOE_BLOCK = 128

kernel_name = 'hybrid_hgrn2_gla_hmoe_stream_step'

def rms_norm(x, g):
    xf = x.astype(jnp.float32)
    y = xf * lax.rsqrt(jnp.mean(xf * xf, axis=-1, keepdims=True) + NORM_EPS)
    return (y * g.astype(jnp.float32)).astype(x.dtype)

def gated_head_norm(o, g, gate):
    o = o.astype(jnp.float32)
    o = o * lax.rsqrt(jnp.mean(o * o, axis=-1, keepdims=True) + NORM_EPS) * g.astype(jnp.float32)
    return o * jax.nn.silu(gate.astype(jnp.float32))

def chunked_gated_linear_attention(q, k, v, log_a, s0):
    B, L, H, dk = q.shape
    dv = v.shape[-1]
    C = min(CHUNK, L)
    n = L // C

    def to_chunks(t):
        return t.astype(jnp.float32).reshape(B, n, C, H, t.shape[-1]).transpose(1, 0, 3, 2, 4)

    causal = jnp.tril(jnp.ones((C, C), dtype=bool))[:, :, None]
    causal_f = causal.astype(jnp.float32)

    def step(S, inp):
        qc, kc, vc, gc = inp
        b = jnp.cumsum(gc, axis=2)
        o_inter = jnp.einsum('bhtk,bhkv->bhtv', qc * jnp.exp(b), S)
        diff = b[:, :, :, None, :] - b[:, :, None, :, :]
        decay = jnp.exp(jnp.where(causal, diff, 0.0)) * causal_f
        scores = jnp.einsum('bhtk,bhsk,bhtsk->bhts', qc, kc, decay)
        o = o_inter + jnp.einsum('bhts,bhsv->bhtv', scores, vc)
        b_last = b[:, :, -1, :]
        S = jnp.exp(b_last)[..., None] * S + jnp.einsum(
            'bhsk,bhsv->bhkv', kc * jnp.exp(b_last[:, :, None, :] - b), vc)
        return S, o

    S, o = lax.scan(step, s0.astype(jnp.float32),
                    (to_chunks(q), to_chunks(k), to_chunks(v), to_chunks(log_a)))
    o = o.transpose(1, 0, 3, 2, 4).reshape(B, L, H, dv)
    return o, S

def token_mixer(h, s_hg, s_gla, lb, w_in, hg_onorm, w_gk2, b_gk, gla_onorm, w_br_a, w_br_b, w_out):
    B, L, _ = h.shape
    split_at = np.cumsum(IN_SPLITS)[:-1].tolist()
    hq, hf, hi, hog, gq, gk, gv, gog, glr, ga, gb = jnp.split(h @ w_in, split_at, axis=-1)

    def heads(t, n_h):
        return t.reshape(B, L, n_h, -1)

    z = heads(hf, HG_HEADS).astype(jnp.float32)
    lbh = lb.reshape(HG_HEADS, HG_DK)
    f = lbh + (1.0 - lbh) * jax.nn.sigmoid(z)
    log_f = jnp.log(jnp.maximum(f, LOG_FLOOR))
    k_hg = (1.0 - lbh) * jax.nn.sigmoid(-z)
    q_hg = jax.nn.silu(heads(hq, HG_HEADS).astype(jnp.float32)) * (HG_DK ** -0.5)
    o_hg, s_hg_new = chunked_gated_linear_attention(q_hg, k_hg, heads(hi, HG_HEADS), log_f, s_hg)
    o_hg = gated_head_norm(o_hg, hg_onorm, heads(hog, HG_HEADS)).reshape(B, L, HG_W).astype(h.dtype)

    log_g = jax.nn.log_sigmoid((glr @ w_gk2 + b_gk).astype(jnp.float32)) / GLA_GATE_NORM
    q_gla = heads(gq, GLA_HEADS).astype(jnp.float32) * (GLA_DK ** -0.5)
    o_gla, s_gla_new = chunked_gated_linear_attention(
        q_gla, heads(gk, GLA_HEADS), heads(gv, GLA_HEADS), heads(log_g, GLA_HEADS), s_gla)
    o_gla = gated_head_norm(o_gla, gla_onorm, heads(gog, GLA_HEADS)).reshape(B, L, GLA_W).astype(h.dtype)

    merged = jax.nn.sigmoid(ga) * (o_hg @ w_br_a) + jax.nn.sigmoid(gb) * (o_gla @ w_br_b)
    return merged @ w_out, s_hg_new.astype(s_hg.dtype), s_gla_new.astype(s_gla.dtype)

def routed_experts(xf, eid, wts, w_gate, w_up, w_down):
    T, D = xf.shape
    A = T * TOPK_IN_GROUP
    flat_e = eid.reshape(A).astype(jnp.int32)
    order = jnp.argsort(flat_e)
    sorted_e = flat_e[order]
    counts = jnp.zeros((N_EXPERTS,), jnp.int32).at[flat_e].add(1)
    starts = jnp.cumsum(counts) - counts
    padded = (counts + MOE_BLOCK - 1) // MOE_BLOCK * MOE_BLOCK
    pad_end = jnp.cumsum(padded)
    pad_start = pad_end - padded
    dest = pad_start[sorted_e] + jnp.arange(A, dtype=jnp.int32) - starts[sorted_e]
    n_blocks = -(-A // MOE_BLOCK) + N_EXPERTS
    buf = jnp.zeros((n_blocks * MOE_BLOCK, D), xf.dtype).at[dest].set(xf[order // TOPK_IN_GROUP])
    block_e = jnp.minimum(
        jnp.searchsorted(pad_end, jnp.arange(n_blocks, dtype=jnp.int32) * MOE_BLOCK, side='right'),
        N_EXPERTS - 1)

    def expert_block(args):
        xb, e = args
        return (jax.nn.silu(xb @ w_gate[e]) * (xb @ w_up[e])) @ w_down[e]

    yb = lax.map(expert_block, (buf.reshape(n_blocks, MOE_BLOCK, D), block_e)).reshape(-1, D)
    y_assign = jnp.zeros((A, D), yb.dtype).at[order].set(yb[dest])
    return jnp.einsum('tkd,tk->td', y_assign.reshape(T, TOPK_IN_GROUP, D), wts.astype(yb.dtype))

def hierarchical_moe(h, w_rg, b_rg, w_re, b_re, w_e_gate, w_e_up, w_e_down):
    B, L, D = h.shape
    xf = h.reshape(B * L, D)
    p_group = jax.nn.softmax((xf @ w_rg + b_rg).astype(jnp.float32), axis=-1)
    gp, gi = lax.top_k(p_group, 1)
    le = (xf @ w_re + b_re).astype(jnp.float32).reshape(-1, N_GROUPS, EXPERTS_PER_GROUP)
    le_sel = jnp.take_along_axis(le, gi[:, :, None], axis=1)[:, 0]
    ve, ie = lax.top_k(jax.nn.softmax(le_sel, axis=-1), TOPK_IN_GROUP)
    wts = gp * ve / jnp.sum(ve, axis=-1, keepdims=True)
    eid = gi * EXPERTS_PER_GROUP + ie
    y = routed_experts(xf, eid, wts, w_e_gate, w_e_up, w_e_down)
    return y.reshape(B, L, D).astype(h.dtype)

def run_trunk(x, c, s_hg_all, s_gla_all, lbs, w_ada, b_ada, norm_mix, norm_ffn, w_in, hg_onorm,
              w_gk2, b_gk, gla_onorm, w_br_a, w_br_b, w_out, w_rg, b_rg, w_re, b_re,
              w_e_gate, w_e_up, w_e_down, norm_final):
    new_hg, new_gla = [], []
    for l in range(DEPTH):
        mod = jax.nn.silu(c) @ w_ada[l] + b_ada[l]
        sh1, sc1, g1, sh2, sc2, g2 = jnp.split(mod[:, None, :], 6, axis=-1)
        h = rms_norm(x, norm_mix[l]) * (1.0 + sc1) + sh1
        m, s_hg, s_gla = token_mixer(h, s_hg_all[l], s_gla_all[l], lbs[l], w_in[l], hg_onorm[l],
                                     w_gk2[l], b_gk[l], gla_onorm[l], w_br_a[l], w_br_b[l], w_out[l])
        x = x + g1 * m
        h = rms_norm(x, norm_ffn[l]) * (1.0 + sc2) + sh2
        x = x + g2 * hierarchical_moe(h, w_rg[l], b_rg[l], w_re[l], b_re[l],
                                      w_e_gate[l], w_e_up[l], w_e_down[l])
        new_hg.append(s_hg)
        new_gla.append(s_gla)
    return rms_norm(x, norm_final), jnp.stack(new_hg), jnp.stack(new_gla)

def setup_inputs(seed: int = 0) -> dict:
    key = jax.random.key(seed)
    ks = jax.random.split(key, 32)
    f32 = jnp.float32

    def nrm(k, shape, scale):
        return jax.random.normal(k, shape, f32) * scale

    D = D_MODEL
    return {
        'x_prompt': nrm(ks[0], (BATCH, SEQ, D), 1.0),
        'x_sample': nrm(ks[1], (DEC_BATCH, DEC_SEQ, D), 1.0),
        'c_prompt': nrm(ks[2], (BATCH, D), 1.0),
        'c_sample': nrm(ks[3], (DEC_BATCH, D), 1.0),
        'state_hgrn': nrm(ks[4], (DEPTH, DEC_BATCH, HG_HEADS, HG_DK, HG_DV), 0.5),
        'state_gla': nrm(ks[5], (DEPTH, DEC_BATCH, GLA_HEADS, GLA_DK, GLA_DV), 2.0),
        'w_ada': nrm(ks[6], (DEPTH, D, 6 * D), 0.5 * D ** -0.5),
        'b_ada': nrm(ks[7], (DEPTH, 6 * D), 0.02),
        'norm_mix': 1.0 + nrm(ks[8], (DEPTH, D), 0.02),
        'norm_ffn': 1.0 + nrm(ks[9], (DEPTH, D), 0.02),
        'w_in': nrm(ks[10], (DEPTH, D, IN_COLS), D ** -0.5),
        'hg_lb': nrm(ks[11], (DEPTH, HG_KW), 0.5),
        'hg_onorm': 1.0 + nrm(ks[12], (DEPTH, HG_DV), 0.02),
        'w_gk2': nrm(ks[13], (DEPTH, GLA_GATE_RANK, GLA_KW), GLA_GATE_RANK ** -0.5),
        'b_gk': nrm(ks[14], (DEPTH, GLA_KW), 0.1),
        'gla_onorm': 1.0 + nrm(ks[15], (DEPTH, GLA_DV), 0.02),
        'w_br_a': nrm(ks[16], (DEPTH, HG_W, D), HG_W ** -0.5),
        'w_br_b': nrm(ks[17], (DEPTH, GLA_W, D), GLA_W ** -0.5),
        'w_out': nrm(ks[18], (DEPTH, D, D), D ** -0.5),
        'w_rg': nrm(ks[19], (DEPTH, D, N_GROUPS), D ** -0.5),
        'b_rg': nrm(ks[20], (DEPTH, N_GROUPS), 0.01),
        'w_re': nrm(ks[21], (DEPTH, D, N_EXPERTS), D ** -0.5),
        'b_re': nrm(ks[22], (DEPTH, N_EXPERTS), 0.01),
        'w_e_gate': nrm(ks[23], (DEPTH, N_EXPERTS, D, D_EXPERT), D ** -0.5),
        'w_e_up': nrm(ks[24], (DEPTH, N_EXPERTS, D, D_EXPERT), D ** -0.5),
        'w_e_down': nrm(ks[25], (DEPTH, N_EXPERTS, D_EXPERT, D), D_EXPERT ** -0.5),
        'norm_final': 1.0 + nrm(ks[26], (D,), 0.02),
    }

def reference(x_prompt, x_sample, c_prompt, c_sample, state_hgrn, state_gla, w_ada, b_ada, norm_mix,
              norm_ffn, w_in, hg_lb, hg_onorm, w_gk2, b_gk, gla_onorm, w_br_a, w_br_b, w_out, w_rg, b_rg,
              w_re, b_re, w_e_gate, w_e_up, w_e_down, norm_final):
    sm = jax.nn.softmax(hg_lb.astype(jnp.float32), axis=0)
    lbs = jnp.clip(jnp.cumsum(sm, axis=0) - sm[0], 0.0, 1.0)
    weights = (w_ada, b_ada, norm_mix, norm_ffn, w_in, hg_onorm, w_gk2, b_gk, gla_onorm, w_br_a, w_br_b,
               w_out, w_rg, b_rg, w_re, b_re, w_e_gate, w_e_up, w_e_down, norm_final)
    bp = x_prompt.shape[0]
    s_hg0 = jnp.zeros((DEPTH, bp, HG_HEADS, HG_DK, HG_DV), x_prompt.dtype)
    s_gla0 = jnp.zeros((DEPTH, bp, GLA_HEADS, GLA_DK, GLA_DV), x_prompt.dtype)
    y_prompt, hg_prompt, gla_prompt = run_trunk(x_prompt, c_prompt, s_hg0, s_gla0, lbs, *weights)
    y_sample, hg_sample, gla_sample = run_trunk(x_sample, c_sample, state_hgrn, state_gla, lbs, *weights)
    return (y_prompt, y_sample, hg_prompt, gla_prompt, hg_sample, gla_sample)


_drawn_inputs = setup_inputs


def setup_inputs(seed=0):
    import zlib

    import numpy as np

    out = dict(_drawn_inputs(seed))
    spreads = {}
    factors = {'state_hgrn': 8.0,
     'norm_ffn': 5.388,
     'hg_onorm': 8.0,
     'gla_onorm': 8.0,
     'b_rg': 8.0,
     'b_re': 8.0,
     'norm_final': 2.776}
    for name, (base, spread) in spreads.items():
        noise = np.random.default_rng([zlib.crc32(name.encode()), seed]).standard_normal(out[name].shape)
        drawn = base * np.exp(spread * noise) if base else spread * noise
        out[name] = __import__('jax').numpy.asarray(drawn.astype(out[name].dtype))
    for name, factor in factors.items():
        out[name] = (out[name] * factor).astype(out[name].dtype)
    return out
```

```python
from contextlib import ExitStack

import numpy as np
import concourse.bass as bass
from concourse import mybir

F32 = mybir.dt.float32
F32R = mybir.dt.float32r
BF16 = mybir.dt.bfloat16
I32 = mybir.dt.int32
U32 = mybir.dt.uint32
ALU = mybir.AluOpType
ACT = mybir.ActivationFunctionType
AX = mybir.AxisListType

P = 128
D = 1024
KD = D // P
T_PROMPT = 1024
T_SAMPLE = 64
T = T_PROMPT + T_SAMPLE
NT = T_PROMPT // P
TILES = [(i * P, P) for i in range(NT)] + [(T_PROMPT, T_SAMPLE)]
COLS = [(0, 364), (364, 364), (728, 360)]
DV = 128
HG_HEADS, HG_DK = 4, 128
GLA_HEADS, GLA_DK, RANK = 4, 64, 16
IN_COLS = 5648
Q_HG, Z_HG, V_HG, G_HG, Q_GLA, K_GLA, V_GLA, G_GLA, LR, GATE_A, GATE_B = (
    0, 512, 1024, 1536, 2048, 2304, 2560, 3072, 3584, 3600, 4624)
EPS = 1e-6
LOG_FLOOR = float(np.log(np.float32(1e-30)))
HALVES = (64, 32, 16, 8, 4, 2, 1)
NL = len(HALVES)
START = 20


def after(n):
    return n + START


def landed(n):
    return n * 16 + START


def arrived(n):
    return n * 16 + 16


def hold(eng, stage):
    eng.sem_inc(stage.held, 1)


class Stage:

    def __init__(self, nc, name):
        self.nc, self.name, self.ctx, self.sems, self.soft = nc, name, ExitStack(), [], []

    def __enter__(self):
        self.ctx.__enter__()
        return self

    def __exit__(self, *a):
        return self.ctx.__exit__(*a)

    def sb(self, name, shape, dtype=F32):
        return self.ctx.enter_context(self.nc.sbuf_tensor(f"{self.name}_{name}", shape, dtype))

    def psum(self, name, shape, dtype=F32):
        return self.ctx.enter_context(self.nc.psum_tensor(f"{self.name}_psum_{name}", shape, dtype))

    def sem(self, name):
        s = self.nc.alloc_semaphore(f"{self.name}_{name}")
        self.sems.append(s)
        return s

    def soft_sem(self, name):
        s = self.nc.alloc_semaphore(f"{self.name}_{name}")
        self.soft.append(s)
        return s

    def block(self):
        self.held = self.sem("held")
        self.ctx.callback(self.clear)
        return self.ctx.enter_context(self.nc.Block())

    def clear(self):
        self.nc.clear_and_free_semaphores(self.sems + self.soft)
        self.nc.all_engine_barrier()


def raise_to_start(sp, stage):
    for s in stage.sems:
        sp.sem_inc(s, START)


def split_matmul(nc, out, lhs, rhs, start, stop):
    nc.tensor.matmul(out, lhs[0], rhs[0], start=start, stop=False)
    nc.tensor.matmul(out, lhs[0], rhs[1], start=False, stop=False)
    return nc.tensor.matmul(out, lhs[1], rhs[0], start=False, stop=stop)


def condition(nc, a, mod_d, h_hi, h_lo, ident):
    AC = 512
    NA = 6 * D // AC
    FIRST = 2 * D // AC
    with Stage(nc, "c") as s:
        c_rows = s.sb("c_rows", [2, D])
        c_tmp = s.sb("c_tmp", [2, D])
        c_sig = s.sb("c_sig", [2, D])
        c_cols = s.sb("c_cols", [P, KD, 2])
        norm8 = s.sb("norm8", [KD, P])
        norm_cols = s.sb("norm_cols", [P, KD])
        b_ada = s.sb("b_ada", [P, NA, P])
        mod = s.sb("mod", [P, NA, P])
        scale = s.sb("scale", [P, KD, 2])
        shift = s.sb("shift", [P, KD, 2])
        w = s.sb("w", [P, 4, KD, AC])
        x = s.sb("x", [P, 4, D])
        xn = s.sb("xn", [P, 2, D])
        junk = s.sb("junk", [P, D])
        stat = s.sb("stat", [P, 2, 8])
        hf = s.sb("hf", [P, 2, KD, P])
        eps = s.sb("eps", [P, 1])
        p_ada = s.psum("ada", [P, 2, 512])
        p_small = s.psum("small", [P, 512])
        p_x = s.psum("x", [P, 2, KD, P])
        p_turn = s.psum("turn", [P, 4, P])
        mod_zero = s.sem("mod_zero")
        ident_ready, zeroed = s.sem("ident_ready"), s.sem("zeroed")
        eps_ready = s.sem("eps_ready")
        small_in, bias_in = s.sem("small_in"), s.sem("bias_in")
        w_in = [s.sem(f"w_in{i}") for i in range(4)]
        x_in = [s.sem(f"x_in{i}") for i in range(4)]
        c_act, c_dve, c_turned, c_ready = s.sem("c_act"), s.sem("c_dve"), s.sem("c_turned"), s.sem("c_ready")
        ada_done, ada_kept = s.sem("ada_done"), s.sem("ada_kept")
        mod_turned, affine_ready = s.sem("mod_turned"), s.sem("affine_ready")
        sumsq, rstd_act, rstd_dve = s.sem("sumsq"), s.sem("rstd_act"), s.sem("rstd_dve")
        x_normed, x_turned, h_full, hi_done, lo_done = (
            s.sem("x_normed"), s.sem("x_turned"), s.sem("h_full"), s.sem("hi_done"), s.sem("lo_done"))
        mod_out = s.sem("mod_out")
        block = s.block()
        w_ada = a["w_ada"].rearrange("l (k p) c -> p (l k) c", p=P)

        def rows_of(t):
            t0, n = TILES[t]
            return (a["x_prompt"][0, t0:t0 + n, :] if t < NT else a["x_sample"][0]), n

        @block.sync
        def _(sp):
            raise_to_start(sp, s)
            sp.dma_start(c_rows[0:1, :], a["c_prompt"]).then_inc(small_in, 16)
            sp.dma_start(c_rows[1:2, :], a["c_sample"]).then_inc(small_in, 16)
            sp.dma_start(norm8[:, :], a["norm_mix"].rearrange("l (k p) -> (l k) p", p=P)).then_inc(small_in, 16)
            for j in range(NA):
                if j >= 4:
                    sp.wait_ge(ada_done, after(j - 3))
                sp.dma_start(w[:, j % 4], w_ada[:, :, j * AC:(j + 1) * AC]).then_inc(w_in[j % 4], 16)
                for t in {1: (0,), 2: (1,), 3: (2,)}.get(j, (j - 1,) if 4 <= j <= NT + 1 else ()):
                    src, n = rows_of(t)
                    if t >= 4:
                        sp.wait_ge(x_normed, after(t - 3))
                    sp.dma_start(x[0:n, t % 4, :], src).then_inc(x_in[t % 4], 16)
            sp.wait_ge(ada_kept, after(NA))
            rows = mod_d.rearrange("g (j r c) -> g j r c", r=4, c=P)
            for r in range(4):
                sp.dma_start(rows[:, :, r, :], mod[32 * r:32 * r + 2]).then_inc(mod_out, 16)
            sp.wait_ge(mod_out, landed(4))

        @block.gpsimd
        def _(pool):
            nc.gpsimd.memset(ident[:], 0.0).then_inc(zeroed, 1)
            pool.wait_ge(zeroed, after(1))
            nc.gpsimd.affine_select(out=ident[:], in_=ident[:], compare_op=ALU.not_equal, fill=1.0, base=0,
                                    pattern=[[-1, P]], channel_multiplier=1).then_inc(ident_ready, 1)
            nc.gpsimd.memset(eps[:], EPS).then_inc(eps_ready, 1)
            nc.gpsimd.memset(mod[:, 0:FIRST, :], 0.0).then_inc(mod_zero, 1)
            for t in range(NT + 1):
                t0, n = TILES[t]
                pool.wait_ge(h_full, after(t + 1))
                nc.gpsimd.tensor_copy(h_hi[:, :, t0:t0 + n], hf[:, t % 2, :, 0:n]).then_inc(hi_done, 1)

        @block.scalar
        def _(act):
            nc.scalar.preload_act_table_set("natural_log_exp_and_others")
            bias = a["b_ada"].rearrange("l (j r c) -> l j r c", r=4, c=P)
            for r in range(4):
                for g in range(2):
                    act.dma_start(b_ada[32 * r + g:32 * r + g + 1], bias[:, :, r, :]).then_inc(bias_in, 16)
            act.wait_ge(small_in, landed(3))
            nc.scalar.activation(c_tmp[:, :], c_rows[:, :], ACT.Abs).then_inc(c_act, 1)
            act.wait_ge(c_act, after(1))
            nc.scalar.activation(c_tmp[:, :], c_tmp[:, :], ACT.Exp, scale=-1.0).then_inc(c_act, 1)
            act.wait_ge(c_act, after(2))
            nc.scalar.activation(c_tmp[:, :], c_tmp[:, :], ACT.Ln, bias=1.0).then_inc(c_act, 1)
            act.wait_ge(c_dve, after(1))
            nc.scalar.activation(c_sig[:, :], c_sig[:, :], ACT.Exp).then_inc(c_act, 1)
            act.wait_ge(eps_ready, after(1))

            def normalise(t):
                src, n = rows_of(t)
                q = stat[0:n, t % 2]
                act.wait_ge(x_in[t % 4], landed(t // 4 + 1))
                if t:
                    act.wait_ge(sumsq, after(t))
                if t >= 2:
                    act.wait_ge(x_normed, after(t - 1))
                nc.scalar.activation(junk[0:n, :], x[0:n, t % 4, :], ACT.Square, scale=float(D) ** -0.5,
                                     accum_out=q[:, 0:1]).then_inc(sumsq, 1)
                act.wait_ge(sumsq, after(t + 1))
                nc.scalar.activation(q[:, 1:2], q[:, 0:1], ACT.Ln, bias=eps[0:n, :]).then_inc(rstd_act, 1)
                act.wait_ge(rstd_act, after(2 * t + 1))
                nc.scalar.activation(q[:, 2:3], q[:, 1:2], ACT.Exp, scale=-0.5).then_inc(rstd_act, 1)

            def modulate(t):
                t0, n = TILES[t]
                g = int(t == NT)
                act.wait_ge(x_turned, after(t + 1))
                if t >= 2:
                    act.wait_ge(lo_done, after(t - 1))
                    act.wait_ge(hi_done, after(t - 1))
                for k in range(KD):
                    m = nc.scalar.activation(hf[:, t % 2, k, 0:n], p_x[:, t % 2, k, 0:n], ACT.Identity,
                                             scale=scale[:, k, g:g + 1], bias=shift[:, k, g:g + 1])
                m.then_inc(h_full, 1)

            normalise(0)
            normalise(1)
            act.wait_ge(affine_ready, after(2))
            for t in range(NT + 1):
                modulate(t)
                if t + 2 <= NT:
                    normalise(t + 2)

        @block.vector
        def _(dve):
            dve.wait_ge(c_act, after(3))
            nc.vector.scalar_tensor_tensor(out=c_sig[:, :], in0=c_rows[:, :], scalar=0.0, in1=c_tmp[:, :],
                                           op0=ALU.min, op1=ALU.subtract).then_inc(c_dve, 1)
            dve.wait_ge(c_act, after(4))
            nc.vector.tensor_tensor(c_sig[:, :], c_sig[:, :], c_rows[:, :], ALU.mult).then_inc(c_dve, 1)
            dve.wait_ge(c_turned, after(1))
            nc.vector.tensor_copy(c_cols[:, :, :], p_small[:, 0:2 * KD].rearrange("p (k g) -> p k g", g=2)).then_inc(c_ready, 1)
            nc.vector.tensor_copy(norm_cols[:, :], p_small[:, 2 * KD:3 * KD]).then_inc(c_ready, 1)

            def keep_ada(j):
                dve.wait_ge(ada_done, after(j + 1))
                for r in range(4):
                    rr = slice(32 * r, 32 * r + 2)
                    m = nc.vector.tensor_tensor(mod[rr, j, :], p_ada[rr, j % 2, 0:P], b_ada[rr, j, :], ALU.add)
                m.then_inc(ada_kept, 1)

            def scale_rows(t):
                n = TILES[t][1]
                q = stat[0:n, t % 2]
                dve.wait_ge(rstd_act, after(2 * t + 2))
                nc.vector.tensor_scalar(q[:, 3:4], q[:, 0:1], EPS, q[:, 2:3], ALU.add, ALU.mult).then_inc(rstd_dve, 1)
                dve.wait_ge(rstd_dve, after(4 * t + 1))
                nc.vector.tensor_scalar(q[:, 4:5], q[:, 3:4], q[:, 2:3], -0.5, ALU.mult, ALU.mult).then_inc(rstd_dve, 1)
                dve.wait_ge(rstd_dve, after(4 * t + 2))
                nc.vector.tensor_scalar(q[:, 5:6], q[:, 4:5], 1.5, q[:, 2:3], ALU.add, ALU.mult).then_inc(rstd_dve, 1)
                dve.wait_ge(rstd_dve, after(4 * t + 3))
                if t >= 2:
                    dve.wait_ge(x_turned, after(t - 1))
                nc.vector.tensor_scalar(xn[0:n, t % 2, :], x[0:n, t % 4, :], q[:, 5:6], None, ALU.mult).then_inc(x_normed, 1)
                nc.vector.tensor_scalar(q[:, 6:7], q[:, 5:6], 1.0, None, ALU.mult).then_inc(rstd_dve, 1)

            def low_half(t):
                t0, n = TILES[t]
                dve.wait_ge(hi_done, after(t + 1))
                nc.vector.tensor_tensor(h_lo[:, :, t0:t0 + n], hf[:, t % 2, :, 0:n],
                                        h_hi[:, :, t0:t0 + n].bitcast(F32), ALU.subtract).then_inc(lo_done, 1)

            dve.wait_ge(mod_zero, after(1))
            dve.wait_ge(bias_in, landed(8))
            for j in range(FIRST):
                keep_ada(j)
            dve.wait_ge(mod_turned, after(1))
            turned = p_turn[:, :, :].rearrange("p j (r g) -> p (j r) g", r=4)[:, :, 0:2]
            nc.vector.tensor_copy(shift[:, :, :], turned[:, 0:KD, :]).then_inc(affine_ready, 1)
            nc.vector.scalar_tensor_tensor(out=scale[:, :, :], in0=turned[:, KD:2 * KD, :], scalar=1.0,
                                           in1=norm_cols[:, :].unsqueeze(2).broadcast_to([P, KD, 2]),
                                           op0=ALU.add, op1=ALU.mult).then_inc(affine_ready, 1)
            scale_rows(0)
            scale_rows(1)
            for t in range(NT + 1):
                if FIRST + t < NA:
                    keep_ada(FIRST + t)
                low_half(t)
                if t + 2 <= NT:
                    scale_rows(t + 2)

        @block.tensor
        def _(pe):
            pe.wait_ge(ident_ready, after(1))
            pe.wait_ge(small_in, landed(3))
            pe.wait_ge(c_dve, after(2))
            for k in range(KD):
                nc.tensor.transpose(p_small[:, 2 * k:2 * k + 2], c_sig[:, k * P:(k + 1) * P], ident[0:2, 0:2])
            nc.tensor.transpose(p_small[:, 2 * KD:3 * KD], norm8[:, :], ident[0:KD, 0:KD]).then_inc(c_turned, 1)
            pe.wait_ge(c_ready, after(2))

            def ada(j):
                pe.wait_ge(w_in[j % 4], landed(j // 4 + 1))
                if j >= 2:
                    pe.wait_ge(ada_kept, after(j - 1))
                for k in range(KD):
                    for r in range(4):
                        m = nc.tensor.matmul(p_ada[32 * r:32 * r + 2, j % 2, 0:P], c_cols[:, k, :],
                                             w[:, j % 4, k, r * P:(r + 1) * P], start=(k == 0), stop=(k == KD - 1))
                m.then_inc(ada_done, 1)

            for j in range(FIRST):
                ada(j)
            pe.wait_ge(ada_kept, after(FIRST))
            for j in range(FIRST):
                m = nc.tensor.transpose(p_turn[:, j, :], mod[:, j, :], ident[:, :])
            m.then_inc(mod_turned, 1)
            for t in range(NT + 1):
                n = TILES[t][1]
                if FIRST + t < NA:
                    ada(FIRST + t)
                pe.wait_ge(x_normed, after(t + 1))
                if t >= 2:
                    pe.wait_ge(h_full, after(t - 1))
                for k in range(KD):
                    m = nc.tensor.transpose(p_x[:, t % 2, k, 0:n], xn[0:n, t % 2, k * P:(k + 1) * P], ident[0:n, 0:n])
                m.then_inc(x_turned, 1)


def mix_heads(nc, a, kind, h_hi, h_lo, ident, mix_d, gate_d, state_out, consts):
    HG = kind == "hg"
    SUB = 1 if HG else 2
    DK = P // SUB
    UNITS = (HG_HEADS if HG else GLA_HEADS // 2)
    NX = 2 if HG else 4
    SCALE = DK ** -0.5
    if HG:
        mine = [("z", Z_HG, P), ("q", Q_HG, P), ("v0", V_HG, P), ("g0", G_HG, P)]
        extra = [(f"x{i}", GATE_A + i * P, NX * P) for i in range(NX)]
    else:
        mine = [("q", Q_GLA, P), ("k", K_GLA, P), ("v0", V_GLA, 2 * P), ("v1", V_GLA + P, 2 * P),
                ("g0", G_GLA, 2 * P), ("g1", G_GLA + P, 2 * P)]
        extra = [(f"x{i}", GATE_B + i * P, NX * P) for i in range(NX)]
    blocks = mine + extra
    NB = len(blocks)
    NC = len(COLS)

    def bank(e):
        return e % 2
    NS = (NT + 1) * SUB
    at = {name: b for b, (name, _, _) in enumerate(blocks)}
    ones, masks, onorm = consts["ones"], consts["masks"], consts["onorm_hg" if HG else "onorm_gla"]
    eps, mean = consts["eps"], consts["mean"]
    with Stage(nc, kind) as s:
        w = s.sb("w", [P, 2, KD, P])
        w_hi = s.sb("w_hi", [P, 2, KD, P], F32R)
        w_lo = s.sb("w_lo", [P, 2, KD, P], F32R)
        q = s.sb("q", [P, T])
        k = s.sb("k", [P, T])
        v = [s.sb(f"v{i}", [P, T]) for i in range(SUB)]
        g = [s.sb(f"g{i}", [P, T]) for i in range(SUB)]
        x = s.sb("x", [P, T])
        t1 = s.sb("t1", [P, T])
        t2 = s.sb("t2", [P, T])
        b = s.sb("b", [P, T])
        lev = s.sb("lev", [P, NL, T])
        qe = s.sb("qe", [P, T])
        eb_last = s.sb("eb_last", [P, NT + 1])
        ke = s.sb("ke", [P, T])
        o = [s.sb(f"o{i}", [P, T]) for i in range(SUB)]
        tok = s.sb("tok", [P, 2, 3, P])
        diag = s.sb("diag", [P, 2, NL, 64])
        sc = s.sb("sc", [P, 2, P])
        state = s.sb("state", [P, 4, DV])
        p_proj = s.psum("proj", [P, 2, 512])
        p_sc = s.psum("sc", [P, 2, 512])
        p_tok = s.psum("tok", [P, 512])
        p_o = s.psum("o", [P, 2, 512])
        p_u = s.psum("u", [P, 512])
        p_ms = p_tok
        if not HG:
            lr_w = s.sb("lr_w", [P, KD, RANK])
            lr_hi = s.sb("lr_hi", [P, KD, RANK], F32R)
            lr_lo = s.sb("lr_lo", [P, KD, RANK], F32R)
            lr = s.sb("lr", [RANK, T])
            gk2 = s.sb("gk2", [RANK, (UNITS + 1) * P])
            gk2_u = s.sb("gk2_u", [RANK, P])
            b_gk = s.sb("b_gk", [P, UNITS + 1])
            b_u = s.sb("b_u", [P, 1])
            gk2_half = s.sem("gk2_half")
            lr_in, lr_split, lr_done, lr_kept = (s.sem("lr_in"), s.sem("lr_split"), s.sem("lr_done"), s.sem("lr_kept"))
            gk2_ready, logit_done, logit_kept = s.sem("gk2_ready"), s.sem("logit_done"), s.sem("logit_kept")
        w_in = [s.sem(f"w_in{i}") for i in range(2)]
        w_hi_done, w_lo_done = s.sem("w_hi_done"), s.sem("w_lo_done")
        proj_done, proj_kept = s.sem("proj_done"), s.sem("proj_kept")
        decay_act, decay_dve, b_done, k_done = s.sem("decay_act"), s.sem("decay_dve"), s.sem("b_done"), s.sem("k_done")
        q_act, q_dve = s.sem("q_act"), s.sem("q_dve")
        lev_diff, lev_exp, lev_half, lev_ready = s.sem("lev_diff"), s.sem("lev_exp"), s.sem("lev_half"), s.sem("lev_ready")
        eb_done, ke_diff, ke_exp, ends_ready = s.sem("eb_done"), s.sem("ke_diff"), s.sem("ke_exp"), s.sem("ends_ready")
        gate_act, gate_dve = s.sem("gate_act"), s.sem("gate_dve")
        gate_out = [s.sem(f"gate_out{i}") for i in range(2)]
        sc_zero = s.sem("sc_zero")
        tok_turned, tok_kept = s.sem("tok_turned"), s.sem("tok_kept")
        sc_done, sc_masked, sc_ready, cross_ready = s.sem("sc_done"), s.sem("sc_masked"), s.sem("sc_ready"), s.sem("cross_ready")
        o_done, o_kept, u_done, state_ready = s.sem("o_done"), s.sem("o_kept"), s.sem("u_done"), s.sem("state_ready")
        state_zero, state_in, state_out_done = s.sem("state_zero"), s.sem("state_in"), s.sem("state_out_done")
        o_sq, ms_done, rstd_ln, rstd_done, o_scaled, o_ready, o_out = (
            s.sem("o_sq"), s.sem("ms_done"), s.sem("rstd_ln"), s.sem("rstd_done"), s.sem("o_scaled"),
            s.sem("o_ready"), s.sem("o_out"))
        block = s.block()
        w_cols = a["w_in"].rearrange("l (k p) c -> p (l k) c", p=P)
        state_prompt, state_sample = state_out
        sample_start = a["state_hgrn" if HG else "state_gla"].rearrange("l b h k v -> (l b h k) v")

        LG = 0 if HG else 1
        PB = NB + LG
        NG = SUB + NX
        NQ = 4 if HG else 0
        ND = 4 if HG else 3
        NDV = 3 if HG else 2

        @block.sync
        def _(sp):
            raise_to_start(sp, s)
            if not HG:
                sp.dma_start(lr_w[:, :, :], w_cols[:, :, LR:LR + RANK]).then_inc(lr_in, 16)
                sp.dma_start(gk2[:, 0:UNITS * P], a["w_gk2"][0]).then_inc(lr_in, 16)
                sp.dma_start(b_gk[:, 0:UNITS], a["b_gk"].rearrange("l (u p) -> p (l u)", p=P), allow_slow_non_contiguous=True).then_inc(lr_in, 16)
            with sp.Fori(0, UNITS) as it:
                for n, (name, base, step) in enumerate(blocks):
                    col = sp.snap(it * step + base)
                    sp.wait_ge(w_lo_done, after(it * NB + n - 1))
                    hold(sp, s)
                    sp.dma_start(w[:, n % 2], w_cols[:, :, bass.ds(col, P)]).then_inc(w_in[n % 2], 16)

        @block.gpsimd
        def _(pool):
            if not HG:
                pool.wait_ge(lr_in, landed(3))
                nc.gpsimd.tensor_copy(lr_hi[:, :, :], lr_w[:, :, :]).then_inc(lr_split, 1)
                pool.wait_ge(lr_split, after(1))
                nc.gpsimd.tensor_tensor(lr_lo[:, :, :], lr_w[:, :, :], lr_hi[:, :, :].bitcast(F32), ALU.subtract).then_inc(lr_split, 1)
            with pool.Fori(0, UNITS) as it:
                for n in range(NB):
                    pool.wait_ge(w_in[n % 2], landed(it * (NB // 2) + n // 2 + 1))
                    pool.wait_ge(proj_done, after((it * PB + LG + n - 1) * NC) if n >= 2 or HG else
                                 after((it * PB + n - 1) * NC))
                    hold(pool, s)
                    nc.gpsimd.tensor_copy(w_hi[:, n % 2], w[:, n % 2]).then_inc(w_hi_done, 1)
                    pool.wait_ge(w_hi_done, after(it * NB + n + 1))
                    nc.gpsimd.tensor_tensor(w_lo[:, n % 2], w[:, n % 2], w_hi[:, n % 2].bitcast(F32),
                                            ALU.subtract).then_inc(w_lo_done, 1)

        @block.tensor
        def _(pe):
            if not HG:
                pe.wait_ge(lr_split, after(2))
                for c, (c0, n) in enumerate(COLS):
                    if c:
                        pe.wait_ge(lr_kept, after(c))
                    for k_ in range(KD):
                        m = split_matmul(nc, p_ms[0:RANK, 0:n], (lr_hi[:, k_, :], lr_lo[:, k_, :]),
                                         (h_hi[:, k_, c0:c0 + n], h_lo[:, k_, c0:c0 + n]), k_ == 0, k_ == KD - 1)
                    m.then_inc(lr_done, 1)
                pe.wait_ge(lr_kept, after(NC))
            with pe.Fori(0, UNITS) as it:
                def logits():
                    pe.wait_ge(gk2_ready, after(it + 1))
                    for c, (c0, n) in enumerate(COLS):
                        pe.wait_ge(proj_kept, after(it * PB * NC + max(c - 1, 0)))
                        nc.tensor.matmul(p_proj[:, c % 2, 0:n], gk2_u[:, :], lr[:, c0:c0 + n],
                                         start=True, stop=True).then_inc(proj_done, 1)

                def project(n_):
                    pe.wait_ge(w_lo_done, after(it * NB + n_ + 1))
                    for c, (c0, n) in enumerate(COLS):
                        e = (LG + n_) * NC + c
                        pe.wait_ge(proj_kept, after(it * PB * NC + max(e - 1, 0)))
                        for k_ in range(KD):
                            m = split_matmul(nc, p_proj[:, bank(e), 0:n], (w_hi[:, n_ % 2, k_, :], w_lo[:, n_ % 2, k_, :]),
                                             (h_hi[:, k_, c0:c0 + n], h_lo[:, k_, c0:c0 + n]), k_ == 0, k_ == KD - 1)
                        m.then_inc(proj_done, 1)

                def turn(i):
                    t0, n = TILES[i]
                    pe.wait_ge(tok_kept, after(it * (NT + 1) + i))
                    hold(pe, s)
                    nc.tensor.transpose(p_tok[0:n, 0:P], ke[:, t0:t0 + n], ident[:, :])
                    for sub in range(SUB):
                        m = nc.tensor.transpose(p_tok[0:n, (1 + sub) * P:(2 + sub) * P], v[sub][:, t0:t0 + n], ident[:, :])
                    m.then_inc(tok_turned, 1)

                def scores(j):
                    i, sub = divmod(j, SUB)
                    t0, n = TILES[i]
                    ch = slice(sub * DK, (sub + 1) * DK)
                    pe.wait_ge(sc_masked, after(it * NS + j - 1))
                    pe.wait_ge(cross_ready, after(it * NT * SUB + min(j, NT * SUB) - 1))
                    hold(pe, s)
                    for h0 in range(0, n, 64):
                        tt = slice(t0 + h0, t0 + h0 + 64)
                        for l in range(NL):
                            left, right = (k, q) if l == 0 else (lev[:, l], lev[:, l])
                            m = nc.tensor.matmul(p_sc[h0:h0 + 64, j % 2, l * 64:(l + 1) * 64], left[ch, tt], right[ch, tt],
                                                 start=True, stop=True)
                    if n == P:
                        m = nc.tensor.matmul(p_sc[0:64, j % 2, NL * 64:NL * 64 + 64], lev[ch, 0, t0:t0 + 64],
                                             lev[ch, 0, t0 + 64:t0 + P], start=True, stop=True)
                    m.then_inc(sc_done, 1)

                def outputs(j):
                    i, sub = divmod(j, SUB)
                    t0, n = TILES[i]
                    ch = slice(sub * DK, (sub + 1) * DK)
                    po = p_o[:, j % 2, 0:n]
                    vt = tok[:, i % 2, 1 + sub, :]
                    if sub == 0:
                        pe.wait_ge(tok_kept, after(it * (NT + 1) + i + 1))
                        if i == 0:
                            pe.wait_ge(state_zero, after(it + 1))
                        elif i < NT:
                            pe.wait_ge(state_ready, after(it * (NT + 1) + i))
                        else:
                            pe.wait_ge(state_in, landed(it + 1))
                            pe.wait_ge(state_ready, after(it * (NT + 1) + i))
                    pe.wait_ge(o_kept, after(it * NS + j - 1))
                    pe.wait_ge(sc_ready, after(it * NS + j + 1))
                    pe.wait_ge(cross_ready, after(it * NT * SUB + min(j + 1, NT * SUB)))
                    hold(pe, s)
                    nc.tensor.matmul(po, state[ch, i % 2 if i < NT else 2, :], qe[ch, t0:t0 + n], start=True, stop=False)
                    nc.tensor.matmul(po, vt[:, :], sc[:, j % 2, 0:n], start=False, stop=True).then_inc(o_done, 1)
                    nc.tensor.matmul(p_u[ch, 0:DV], tok[0:n, i % 2, 0, ch], vt[0:n, :], start=True, stop=True).then_inc(u_done, 1)

                if not HG:
                    logits()
                for n_ in range(NB - 1):
                    project(n_)
                pe.wait_ge(lev_ready, after((it + 1) * NL))
                pe.wait_ge(ends_ready, after(2 * it + 2))
                pe.wait_ge(proj_kept, after((it * PB + LG + at[f"v{SUB - 1}"] + 1) * NC))
                turn(0)
                scores(0)
                for j in range(NS):
                    if j + 1 < NS:
                        if (j + 1) % SUB == 0:
                            turn((j + 1) // SUB)
                        scores(j + 1)
                    outputs(j)
                project(NB - 1)
                for sub in range(SUB):
                    pe.wait_ge(o_sq, after(it * SUB + sub + 1))
                    for c, (c0, n) in enumerate(COLS):
                        pe.wait_ge(rstd_ln, after((it * SUB + sub) * NC + c))
                        nc.tensor.matmul(p_ms[:, 0:n], mean[:, :], ke[:, c0:c0 + n], start=True, stop=True).then_inc(ms_done, 1)

        chains = [(f"g{i}", g[i], t1) for i in range(SUB)] + [(f"x{i}", x, (t2, t1)[i % 2]) for i in range(NX)]

        def keep_output(act, it, j):
            i, sub = divmod(j, SUB)
            t0, n = TILES[i]
            act.wait_ge(o_done, after(it * NS + j + 1))
            act.wait_ge(o_out, landed(it * SUB))
            nc.scalar.activation(o[sub][:, t0:t0 + n], p_o[:, j % 2, 0:n], ACT.Copy).then_inc(o_kept, 1)

        @block.scalar
        def _(act):
            nc.scalar.preload_act_table_set("natural_log_exp_and_others")
            if not HG:
                for c, (c0, n) in enumerate(COLS):
                    act.wait_ge(lr_done, after(c + 1))
                    nc.scalar.activation(lr[:, c0:c0 + n], p_ms[0:RANK, 0:n], ACT.Copy).then_inc(lr_kept, 1)
            with act.Fori(0, UNITS) as it:
                def keep(pb, dst, func=ACT.Copy, **kw):
                    for c, (c0, n) in enumerate(COLS):
                        e = pb * NC + c
                        act.wait_ge(proj_done, after(it * PB * NC + e + 1))
                        nc.scalar.activation(dst[:, c0:c0 + n], p_proj[:, bank(e), 0:n], func, **kw).then_inc(proj_kept, 1)

                def log_one_plus(src, dst, sem, n0, per):
                    nc.scalar.activation(dst[:, :], src[:, :], ACT.Abs).then_inc(sem, 1)
                    act.wait_ge(sem, after(it * per + n0 + 1))
                    nc.scalar.activation(dst[:, :], dst[:, :], ACT.Exp, scale=-1.0).then_inc(sem, 1)
                    act.wait_ge(sem, after(it * per + n0 + 2))
                    nc.scalar.activation(dst[:, :], dst[:, :], ACT.Ln, bias=1.0).then_inc(sem, 1)

                def level(l):
                    act.wait_ge(lev_diff, after(2 * (it * NL + l) + 2))
                    end = T_PROMPT if HALVES[l] == 64 else T
                    nc.scalar.activation(lev[:, l, 0:end], lev[:, l, 0:end], ACT.Exp).then_inc(lev_exp, 1)

                def gate_chain(n_):
                    name, src, tmp = chains[n_]
                    xi = n_ - SUB
                    act.wait_ge(proj_kept, after((it * PB + LG + at[name] + 1) * NC))
                    if xi >= 0:
                        act.wait_ge(gate_out[xi % 2], landed(it * (NX // 2) + xi // 2))
                    elif n_ > 0:
                        act.wait_ge(gate_dve, after((2 * SUB + NX) * it + 2 * n_))
                    log_one_plus(src, tmp, gate_act, 4 * n_, 4 * NG)
                    act.wait_ge(gate_dve, after((2 * SUB + NX) * it + (2 * n_ + 1 if n_ < SUB else 2 * SUB + xi + 1)))
                    nc.scalar.activation(tmp[:, :], tmp[:, :], ACT.Exp).then_inc(gate_act, 1)
                    if xi >= 0:
                        row = act.snap(it * NX + xi + (0 if HG else 8))
                        act.wait_ge(gate_act, after(4 * NG * it + 4 * n_ + 4))
                        act.dma_start(gate_d[bass.ds(row, 1), :, :].rearrange("a p t -> (a p) t"), tmp[:, :]).then_inc(gate_out[xi % 2], 16)

                row0 = act.snap(it * P)
                if HG:
                    keep(at["z"], k)
                    act.wait_ge(proj_kept, after((it * PB + 1) * NC))
                    act.wait_ge(gate_out[1], landed(it * (NX // 2)))
                    log_one_plus(k, t1, decay_act, 0, ND)
                    act.wait_ge(decay_dve, after(it * NDV + 3))
                    nc.scalar.activation(k[:, :], k[:, :], ACT.Exp).then_inc(decay_act, 1)
                    keep(at["q"], q)
                    act.wait_ge(proj_kept, after((it * PB + 2) * NC))
                    log_one_plus(q, qe, q_act, 0, NQ)
                else:
                    act.wait_ge(gk2_ready, after(it + 1))
                    act.wait_ge(gate_out[0], landed(it * (NX // 2)))
                    keep(0, t2, ACT.Identity, bias=b_u[:, :])
                    act.wait_ge(proj_kept, after(it * PB * NC + NC))
                    act.wait_ge(gate_out[1], landed(it * (NX // 2)))
                    log_one_plus(t2, t1, decay_act, 0, ND)
                    keep(LG + at["q"], q, scale=SCALE)
                    keep(LG + at["k"], k)
                act.wait_ge(state_out_done, landed(2 * it))
                act.dma_start(state[:, 2, :], sample_start[bass.ds(row0, P), :]).then_inc(state_in, 16)
                for l in range(4):
                    level(l)
                if HG:
                    act.wait_ge(q_dve, after(2 * it + 1))
                    nc.scalar.activation(qe[:, :], qe[:, :], ACT.Exp).then_inc(q_act, 1)
                keep(LG + at["v0"], v[0])
                for l in range(4, NL):
                    level(l)
                act.wait_ge(ke_diff, after(2 * it + 2))
                nc.scalar.activation(ke[:, :], ke[:, :], ACT.Exp).then_inc(ke_exp, 1)
                act.wait_ge(b_done, after((NT + 1) * (it + 1)))
                if HG:
                    act.wait_ge(q_dve, after(2 * it + 2))
                nc.scalar.activation(qe[:, :], b[:, :], ACT.Exp).then_inc(eb_done, 1)
                nc.scalar.activation(eb_last[:, 0:NT], b[:, P - 1:T_PROMPT:P], ACT.Exp).then_inc(eb_done, 1)
                nc.scalar.activation(eb_last[:, NT:NT + 1], b[:, T - 1:T], ACT.Exp).then_inc(eb_done, 1)
                for i in range(1, SUB):
                    keep(LG + at[f"v{i}"], v[i])
                for i in range(SUB):
                    keep(LG + at[f"g{i}"], g[i])
                for i in range(SUB):
                    gate_chain(i)
                for i in range(NX - 1):
                    if i:
                        act.wait_ge(gate_dve, after((2 * SUB + NX) * it + 2 * SUB + i))
                    else:
                        act.wait_ge(gate_dve, after((2 * SUB + NX) * it))
                    keep(LG + at[f"x{i}"], x)
                    gate_chain(SUB + i)
                for j in range(NS):
                    i, sub = divmod(j, SUB)
                    t0, n = TILES[i]
                    if sub == 0:
                        act.wait_ge(tok_turned, after(it * (NT + 1) + i + 1))
                        act.wait_ge(u_done, after(it * NS + (i - 1) * SUB))
                        nc.scalar.activation(tok[0:n, i % 2, 0:1 + SUB, :], p_tok[0:n, 0:(1 + SUB) * P].rearrange("p (a c) -> p a c", c=P),
                                             ACT.Copy).then_inc(tok_kept, 1)
                    if j:
                        keep_output(act, it, j - 1)
                keep_output(act, it, NS - 1)
                for sub in range(SUB):
                    if sub == 0:
                        act.wait_ge(o_kept, after((it + 1) * NS))
                    else:
                        act.wait_ge(ms_done, after((it * SUB + sub) * NC))
                    nc.scalar.activation(ke[:, :], o[sub][:, :], ACT.Square).then_inc(o_sq, 1)
                    if sub == 0:
                        act.wait_ge(gate_dve, after((2 * SUB + NX) * it + 2 * SUB + NX - 1))
                        keep(LG + at[f"x{NX - 1}"], x)
                    else:
                        act.wait_ge(o_scaled, after(it * SUB + sub))
                    for c, (c0, n) in enumerate(COLS):
                        act.wait_ge(ms_done, after((it * SUB + sub) * NC + c + 1))
                        nc.scalar.activation(qe[:, c0:c0 + n], p_ms[:, 0:n], ACT.Ln, bias=eps[:, :]).then_inc(rstd_ln, 1)
                    act.wait_ge(rstd_ln, after((it * SUB + sub + 1) * NC))
                    nc.scalar.activation(qe[:, :], qe[:, :], ACT.Exp, scale=-0.5).then_inc(rstd_done, 1)
                gate_chain(SUB + NX - 1)
                for sub in range(SUB):
                    row = act.snap(it * SUB + sub + (0 if HG else HG_HEADS))
                    act.wait_ge(o_ready, after(it * SUB + sub + 1))
                    act.dma_start(mix_d[bass.ds(row, 1), :, :].rearrange("a p t -> (a p) t"), o[sub][:, :]).then_inc(o_out, 16)
                for i, (dst, slot, last) in enumerate(((state_prompt, 0, NT), (state_sample, 3, NT + 1))):
                    act.wait_ge(state_ready, after(it * (NT + 1) + last))
                    act.dma_start(dst[bass.ds(row0, P), :], state[:, slot, :]).then_inc(state_out_done, 16)
            act.wait_ge(state_out_done, landed(2 * UNITS))
            act.wait_ge(o_out, landed(UNITS * SUB))
            for p_ in range(2):
                act.wait_ge(gate_out[p_], landed(UNITS * NX // 2))

        @block.vector
        def _(dve):
            nc.vector.memset(sc[:, :, :], 0.0).then_inc(sc_zero, 1)
            dve.wait_ge(sc_zero, after(1))
            if not HG:
                nc.vector.memset(gk2[:, UNITS * P:], 0.0).then_inc(gk2_half, 1)
                nc.vector.memset(b_gk[:, UNITS:], 0.0).then_inc(gk2_half, 1)
                dve.wait_ge(lr_in, landed(3))
                nc.vector.tensor_copy(gk2_u[:, :], gk2[:, 0:P]).then_inc(gk2_half, 1)
                dve.wait_ge(gk2_half, after(3))
                nc.vector.tensor_copy(b_u[:, :], b_gk[:, 0:1]).then_inc(gk2_ready, 1)
            with dve.Fori(0, UNITS) as it:
                V = nc.vector
                if HG:
                    dve.wait_ge(decay_act, after(it * ND + 3))
                    V.scalar_tensor_tensor(out=t1[:, :], in0=k[:, :], scalar=0.0, in1=t1[:, :],
                                           op0=ALU.min, op1=ALU.subtract).then_inc(decay_dve, 1)
                    dve.wait_ge(decay_dve, after(it * NDV + 1))
                    dve.wait_ge(gate_out[0], landed(it * (NX // 2)))
                    V.tensor_scalar(t2[:, :], t1[:, :], LOG_FLOOR, None, ALU.max).then_inc(decay_dve, 1)
                    V.tensor_tensor(k[:, :], t1[:, :], k[:, :], ALU.subtract).then_inc(decay_dve, 1)
                    dve.wait_ge(decay_dve, after(it * NDV + 2))
                else:
                    dve.wait_ge(decay_act, after(it * ND + 3))
                    V.scalar_tensor_tensor(out=t1[:, :], in0=t2[:, :], scalar=0.0, in1=t1[:, :],
                                           op0=ALU.min, op1=ALU.subtract).then_inc(decay_dve, 1)
                    dve.wait_ge(decay_dve, after(it * NDV + 1))
                    V.tensor_scalar(t2[:, :], t1[:, :], 1.0 / 16.0, None, ALU.mult).then_inc(decay_dve, 1)
                    dve.wait_ge(decay_dve, after(it * NDV + 2))
                for t0, n in TILES:
                    V.tensor_tensor_scan(b[:, t0:t0 + n], ones[:, 0:n], t2[:, t0:t0 + n], 0.0, ALU.mult, ALU.add).then_inc(b_done, 1)
                dve.wait_ge(b_done, after((NT + 1) * (it + 1)))
                for l, h in enumerate(HALVES):
                    end = T_PROMPT if h == 64 else T
                    bb = b[:, 0:end].rearrange("p (n c h) -> p n c h", c=2, h=h)
                    ll = lev[:, l, 0:end].rearrange("p (n c h) -> p n c h", c=2, h=h)
                    r = bb[:, :, 0, h - 1:h].broadcast_to([P, end // (2 * h), h])
                    V.tensor_tensor(ll[:, :, 0, :], r, bb[:, :, 0, :], ALU.subtract).then_inc(lev_diff, 1)
                    V.tensor_tensor(ll[:, :, 1, :], bb[:, :, 1, :], r, ALU.subtract).then_inc(lev_diff, 1)
                for c0, n, m in ((0, P, NT), (T_PROMPT, T_SAMPLE, 1)):
                    bb = b[:, c0:c0 + n * m].rearrange("p (m n) -> p m n", n=n)
                    V.tensor_tensor(ke[:, c0:c0 + n * m].rearrange("p (m n) -> p m n", n=n),
                                    bb[:, :, n - 1:n].broadcast_to([P, m, n]), bb, ALU.subtract).then_inc(ke_diff, 1)
                if HG:
                    dve.wait_ge(q_act, after(it * NQ + 3))
                    V.scalar_tensor_tensor(out=qe[:, :], in0=q[:, :], scalar=0.0, in1=qe[:, :],
                                           op0=ALU.min, op1=ALU.subtract).then_inc(q_dve, 1)
                    dve.wait_ge(q_act, after(it * NQ + 4))
                    V.scalar_tensor_tensor(out=q[:, :], in0=q[:, :], scalar=SCALE, in1=qe[:, :],
                                           op0=ALU.mult, op1=ALU.mult).then_inc(q_dve, 1)
                    dve.wait_ge(q_dve, after(2 * it + 2))
                    dve.wait_ge(decay_act, after((it + 1) * ND))
                else:
                    dve.wait_ge(proj_kept, after((it * PB + LG + at["k"] + 1) * NC))
                for l, h in enumerate(HALVES):
                    end = T_PROMPT if h == 64 else T
                    ll = lev[:, l, 0:end].rearrange("p (n c h) -> p n c h", c=2, h=h)
                    dve.wait_ge(lev_exp, after(it * NL + l + 1))
                    V.tensor_tensor(ll[:, :, 0, :], ll[:, :, 0, :], k[:, 0:end].rearrange("p (n c h) -> p n c h", c=2, h=h)[:, :, 0, :],
                                    ALU.mult).then_inc(lev_half, 1)
                    V.tensor_tensor(ll[:, :, 1, :], ll[:, :, 1, :], q[:, 0:end].rearrange("p (n c h) -> p n c h", c=2, h=h)[:, :, 1, :],
                                    ALU.mult).then_inc(lev_ready, 1)
                dve.wait_ge(ke_exp, after(it + 1))
                V.tensor_tensor(ke[:, :], ke[:, :], k[:, :], ALU.mult).then_inc(ends_ready, 1)
                dve.wait_ge(eb_done, after(3 * it + 3))
                V.tensor_tensor(qe[:, :], qe[:, :], q[:, :], ALU.mult).then_inc(ends_ready, 1)

                def gate_half(n_):
                    name, src, tmp = chains[n_]
                    per = 4 * NG
                    dve.wait_ge(gate_act, after(per * it + 4 * n_ + 3))
                    V.scalar_tensor_tensor(out=tmp[:, :], in0=src[:, :], scalar=0.0, in1=tmp[:, :],
                                           op0=ALU.min, op1=ALU.subtract).then_inc(gate_dve, 1)
                    if n_ < SUB:
                        dve.wait_ge(gate_act, after(per * it + 4 * n_ + 4))
                        V.tensor_tensor(src[:, :], src[:, :], tmp[:, :], ALU.mult).then_inc(gate_dve, 1)

                for n_ in range(NG - 1):
                    gate_half(n_)

                def mask(j):
                    i, sub = divmod(j, SUB)
                    n = TILES[i][1]
                    dve.wait_ge(sc_done, after(it * NS + j + 1))
                    V.tensor_tensor(diag[0:n, j % 2], p_sc[0:n, j % 2, 0:NL * 64].rearrange("p (l t) -> p l t", t=64),
                                    masks[0:n], ALU.mult).then_inc(sc_masked, 1)
                    dve.wait_ge(sc_masked, after(it * NS + j + 1))
                    dve.wait_ge(o_done, after(it * NS + j - 1))
                    if n == P:
                        V.tensor_copy(sc[0:64, j % 2, 64:P], p_sc[0:64, j % 2, NL * 64:NL * 64 + 64]).then_inc(cross_ready, 1)
                    for h0 in range(0, n, 64):
                        red = V.tensor_reduce(sc[h0:h0 + 64, j % 2, h0:h0 + 64], diag[h0:h0 + 64, j % 2].rearrange("p l t -> p t l"),
                                              AX.X, ALU.add)
                    red.then_inc(sc_ready, 1)

                dve.wait_ge(state_out_done, landed(2 * it))
                V.memset(state[:, 0, :], 0.0).then_inc(state_zero, 1)
                mask(0)
                for j in range(NS):
                    if j + 1 < NS:
                        mask(j + 1)
                    i, sub = divmod(j, SUB)
                    if sub == SUB - 1:
                        src, dst = (i % 2, (i + 1) % 2) if i < NT else (2, 3)
                        dve.wait_ge(u_done, after(it * NS + j + 1))
                        if i >= 1:
                            dve.wait_ge(state_ready, after(it * (NT + 1) + i))
                        if i == NT:
                            dve.wait_ge(state_in, landed(it + 1))
                        V.scalar_tensor_tensor(out=state[:, dst, :], in0=state[:, src, :], scalar=eb_last[:, i:i + 1],
                                               in1=p_u[:, 0:DV], op0=ALU.mult, op1=ALU.add).then_inc(state_ready, 1)
                if not HG:
                    dve.wait_ge(proj_kept, after((it * PB + 1) * NC))
                    V.tensor_copy(gk2_u[:, :], gk2[:, bass.ds(it * P + P, P)]).then_inc(gk2_half, 1)
                    dve.wait_ge(gk2_half, after(it + 4))
                    V.tensor_copy(b_u[:, :], b_gk[:, bass.ds(it + 1, 1)]).then_inc(gk2_ready, 1)
                for sub in range(SUB):
                    dve.wait_ge(rstd_done, after(it * SUB + sub + 1))
                    V.tensor_tensor(o[sub][:, :], o[sub][:, :], qe[:, :], ALU.mult).then_inc(o_scaled, 1)
                    dve.wait_ge(o_scaled, after(it * SUB + sub + 1))
                    V.scalar_tensor_tensor(out=o[sub][:, :], in0=o[sub][:, :], scalar=onorm[:, 0:1], in1=g[sub][:, :],
                                           op0=ALU.mult, op1=ALU.mult).then_inc(o_ready, 1)
                gate_half(NG - 1)


def merge(nc, a, mix_d, gate_d, m_hi, m_lo):
    NC, K = len(COLS), 4
    with Stage(nc, "m") as s:
        mix = s.sb("mix", [P, 3, T])
        mix_hi, mix_lo = s.sb("mix_hi", [P, 2 * K, T], F32R), s.sb("mix_lo", [P, 2 * K, T], F32R)
        w = s.sb("w", [P, 2, 2 * K, P])
        w_hi, w_lo = s.sb("w_hi", [P, 2, 2 * K, P], F32R), s.sb("w_lo", [P, 2, 2 * K, P], F32R)
        gate = s.sb("gate", [P, 2, 2, T])
        merged = s.sb("merged", [P, 2, T])
        part = s.sb("part", [P, 2, 512])
        p_a, p_b = s.psum("a", [P, 2, 512]), s.psum("b", [P, 2, 512])
        mix_in = [s.sem(f"mix_in{i}") for i in range(3)]
        mix_hi_done, mix_lo_done = s.sem("mix_hi_done"), s.sem("mix_lo_done")
        w_in, gate_in = [s.sem(f"w_in{i}") for i in range(2)], [s.sem(f"gate_in{i}") for i in range(2)]
        w_hi_done, w_lo_done = s.sem("w_hi_done"), s.sem("w_lo_done")
        a_done, b_done, a_gated, b_gated, piece_done = (
            s.sem("a_done"), s.sem("b_done"), s.sem("a_gated"), s.sem("b_gated"), s.sem("piece_done"))
        m_hi_done, m_lo_done = s.sem("m_hi_done"), s.sem("m_lo_done")
        block = s.block()
        w_a = a["w_br_a"].rearrange("l (k p) c -> p (l k) c", p=P)
        w_b = a["w_br_b"].rearrange("l (k p) c -> p (l k) c", p=P)

        @block.sync
        def _(sp):
            raise_to_start(sp, s)
            with sp.Fori(0, KD // 2) as i:
                for j in range(2):
                    c0 = sp.snap(i * (2 * P) + j * P)
                    row_a, row_b = sp.snap(i * 2 + j), sp.snap(i * 2 + j + KD)
                    sp.wait_ge(w_lo_done, after(2 * i + j - 1))
                    hold(sp, s)
                    sp.dma_start(w[:, j, 0:K], w_a[:, :, bass.ds(c0, P)]).then_inc(w_in[j], 16)
                    sp.dma_start(w[:, j, K:2 * K], w_b[:, :, bass.ds(c0, P)]).then_inc(w_in[j], 16)
                    sp.wait_ge(b_gated, after((2 * i + j - 1) * NC))
                    hold(sp, s)
                    for half, row in enumerate((row_a, row_b)):
                        sp.dma_start(gate[:, j, half, :],
                                     gate_d[bass.ds(row, 1), :, :].rearrange("a p t -> (a p) t")).then_inc(gate_in[j], 16)

        @block.gpsimd
        def _(pool):
            with pool.Fori(0, KD // 2) as i:
                for j in range(2):
                    pool.wait_ge(w_in[j], landed(2 * i + 2))
                    pool.wait_ge(b_done, after((2 * i + j - 1) * NC))
                    hold(pool, s)
                    nc.gpsimd.tensor_copy(w_hi[:, j], w[:, j]).then_inc(w_hi_done, 1)
                    pool.wait_ge(w_hi_done, after(2 * i + j + 1))
                    hold(pool, s)
                    nc.gpsimd.tensor_tensor(w_lo[:, j], w[:, j], w_hi[:, j].bitcast(F32), ALU.subtract).then_inc(w_lo_done, 1)

        @block.scalar
        def _(act):
            for u in range(3):
                act.dma_start(mix[:, u, :], mix_d[u]).then_inc(mix_in[u], 16)
            for u in range(2 * K):
                act.wait_ge(mix_in[u % 3], landed(u // 3 + 1))
                nc.scalar.activation(mix_hi[:, u, :], mix[:, u % 3, :], ACT.Copy).then_inc(mix_hi_done, 1)
                if 1 <= u and u + 2 < 2 * K:
                    act.wait_ge(mix_lo_done, after(u))
                    act.dma_start(mix[:, (u + 2) % 3, :], mix_d[u + 2]).then_inc(mix_in[(u + 2) % 3], 16)
            with act.Fori(0, KD // 2) as i:
                for j in range(2):
                    act.wait_ge(piece_done, after((2 * i + j + 1) * NC))
                    nc.scalar.activation(m_hi[:, bass.ds(i * 2 + j, 1), :].rearrange("p a t -> p (a t)"), merged[:, j, :],
                                         ACT.Copy).then_inc(m_hi_done, 1)

        @block.vector
        def _(dve):
            V = nc.vector
            for u in range(2 * K):
                dve.wait_ge(mix_hi_done, after(u + 1))
                V.tensor_tensor(mix_lo[:, u, :], mix[:, u % 3, :], mix_hi[:, u, :].bitcast(F32), ALU.subtract).then_inc(mix_lo_done, 1)
            with dve.Fori(0, KD // 2) as i:
                for j in range(2):
                    n0 = (2 * i + j) * NC
                    dve.wait_ge(gate_in[j], landed(2 * i + 2))
                    for c, (c0, n) in enumerate(COLS):
                        r = part[:, c % 2, 0:n]
                        dve.wait_ge(a_done, after(n0 + c + 1))
                        V.tensor_tensor(merged[:, j, c0:c0 + n], gate[:, j, 0, c0:c0 + n], p_a[:, c % 2, 0:n], ALU.mult).then_inc(a_gated, 1)
                        dve.wait_ge(b_done, after(n0 + c + 1))
                        V.tensor_tensor(r, gate[:, j, 1, c0:c0 + n], p_b[:, c % 2, 0:n], ALU.mult).then_inc(b_gated, 1)
                        dve.wait_ge(b_gated, after(n0 + c + 1))
                        V.tensor_tensor(merged[:, j, c0:c0 + n], merged[:, j, c0:c0 + n], r, ALU.add).then_inc(piece_done, 1)
                    dve.wait_ge(m_hi_done, after(2 * i + j + 1))
                    V.tensor_tensor(m_lo[:, bass.ds(i * 2 + j, 1), :].rearrange("p a t -> p (a t)"), merged[:, j, :],
                                    m_hi[:, bass.ds(i * 2 + j, 1), :].rearrange("p a t -> p (a t)").bitcast(F32),
                                    ALU.subtract).then_inc(m_lo_done, 1)

        @block.tensor
        def _(pe):
            with pe.Fori(0, KD // 2) as i:
                for j in range(2):
                    n0 = (2 * i + j) * NC
                    pe.wait_ge(w_lo_done, after(2 * i + j + 1))
                    for c, (c0, n) in enumerate(COLS):
                        pe.wait_ge(b_gated, after(n0 + max(c - 1, 0)))
                        for half, p_x, done in ((0, p_a, a_done), (K, p_b, b_done)):
                            for k in range(half, half + K):
                                if j == 0 and c == 0:
                                    pe.wait_ge(mix_lo_done, after(k + 1))
                                m = split_matmul(nc, p_x[:, c % 2, 0:n], (w_hi[:, j, k, :], w_lo[:, j, k, :]),
                                                 (mix_hi[:, k, c0:c0 + n], mix_lo[:, k, c0:c0 + n]), k == half, k == half + K - 1)
                            m.then_inc(done, 1)


def rstd_newton(V, eng, q, done, n0):
    V.tensor_scalar(q[:, 3:4], q[:, 0:1], EPS, q[:, 2:3], ALU.add, ALU.mult).then_inc(done, 1)
    eng.wait_ge(done, after(n0 + 1))
    V.tensor_scalar(q[:, 4:5], q[:, 3:4], q[:, 2:3], -0.5, ALU.mult, ALU.mult).then_inc(done, 1)
    eng.wait_ge(done, after(n0 + 2))
    V.tensor_scalar(q[:, 5:6], q[:, 4:5], 1.5, q[:, 2:3], ALU.add, ALU.mult).then_inc(done, 1)
    eng.wait_ge(done, after(n0 + 3))


def out_router(nc, a, mod_d, x2_d, h2_d, m_hi, m_lo, ident, consts, route):
    NTT = NT + 1
    eid, pos, wts, m_all = route["eid"], route["pos"], route["wts"], route["m_all"]
    with Stage(nc, "o") as s:
        w = s.sb("w", [P, 4, D])
        w_hi, w_lo = s.sb("w_hi", [P, KD, D], F32R), s.sb("w_lo", [P, KD, D], F32R)
        rows = s.sb("rows", [P, 2, 3, D])
        x, x2, h2 = s.sb("x", [P, 2, D]), s.sb("x2", [P, 2, D]), s.sb("h2", [P, 2, D])
        hT = s.sb("hT", [P, KD, P])
        stat = s.sb("stat", [P, 2, 8])
        w_r, b_r = s.sb("w_r", [P, KD, 36]), s.sb("b_r", [P, 36])
        gl = s.sb("gl", [P, 8])
        le, picked, sel = s.sb("le", [P, 4, 8]), s.sb("picked", [P, 4, 8]), s.sb("sel", [P, 8])
        top, sub_top = s.sb("top", [P, 8]), s.sb("sub_top", [P, 8])
        top_i, sub_i = s.sb("top_i", [P, 8], U32), s.sb("sub_i", [P, 8], U32)
        f, one_g, junk = s.sb("f", [P, 16]), s.sb("one_g", [P, 4]), s.sb("junk", [P, 8])
        hot, ranked, m_tile = s.sb("hot", [P, 2, 32]), s.sb("ranked", [P, 2, 32]), s.sb("m_tile", [P, 32], BF16)
        tri_b, ones_b = s.sb("tri_b", [P, P], BF16), s.sb("ones_b", [P, P], BF16)
        p_m, p_h = s.psum("m", [P, 2, D]), s.psum("h", [P, KD, P])
        p_l, p_r = s.psum("l", [P, 512]), s.psum("r", [P, 512])
        w_in = [s.sem(f"w_in{i}") for i in range(4)]
        x_in, x2_out, h2_out = ([s.sem(f"{name}{i}") for i in range(2)] for name in ("x_in", "x2_out", "h2_out"))
        w_hi_done, w_lo_done = s.sem("w_hi_done"), s.sem("w_lo_done")
        rows_in, rows_scaled, small_in, ready = s.sem("rows_in"), s.sem("rows_scaled"), s.sem("small_in"), s.sem("ready")
        m_done, m_gated, x2_ready, sumsq, rstd_act, rstd_dve = (
            s.sem("m_done"), s.sem("m_gated"), s.sem("x2_ready"), s.sem("sumsq"), s.sem("rstd_act"), s.sem("rstd_dve"))
        h2_scaled, h2_ready, h2_turned, hT_ready, logits_done = (
            s.sem("h2_scaled"), s.sem("h2_ready"), s.sem("h2_turned"), s.sem("hT_ready"), s.sem("logits_done"))
        routed, gmax_ready, gsum_ready, diff_ready, ratio_ready = (
            s.sem("routed"), s.sem("gmax_ready"), s.sem("gsum_ready"), s.sem("diff_ready"), s.sem("ratio_ready"))
        hot_ready, rank_done, m_all_ready = s.sem("hot_ready"), s.sem("rank_done"), s.sem("m_all_ready")
        block = s.block()
        w_out = a["w_out"].rearrange("l (k p) c -> p (l k) c", p=P)

        def x_rows(t):
            t0, n = TILES[t]
            return (a["x_prompt"][0, t0:t0 + n, :] if t < NT else a["x_sample"][0]), n

        @block.sync
        def _(sp):
            raise_to_start(sp, s)
            for k in range(KD):
                if k >= 4:
                    sp.wait_ge(w_lo_done, after(k - 3))
                sp.dma_start(w[:, k % 4, :], w_out[:, k, :]).then_inc(w_in[k % 4], 16)
            for g in range(2):
                for i, part in enumerate((2, 4, 3)):
                    sp.dma_start(rows[:, g, i, :], mod_d[g:g + 1, part * D:(part + 1) * D].partition_broadcast(P)).then_inc(rows_in, 16)
            sp.dma_start(x2[:, 0, :], a["norm_ffn"].partition_broadcast(P)).then_inc(rows_in, 16)
            sp.dma_start(w_r[:, :, 0:4], a["w_rg"].rearrange("l (k p) c -> p (l k) c", p=P)).then_inc(small_in, 16)
            sp.dma_start(w_r[:, :, 4:36], a["w_re"].rearrange("l (k p) c -> p (l k) c", p=P)).then_inc(small_in, 16)
            sp.dma_start(b_r[:, 0:4], a["b_rg"].partition_broadcast(P)).then_inc(small_in, 16)
            sp.dma_start(b_r[:, 4:36], a["b_re"].partition_broadcast(P)).then_inc(small_in, 16)

            def store(t):
                t0, n = TILES[t]
                sp.wait_ge(x2_ready, after(t + 1))
                sp.dma_start(x2_d[t0:t0 + n, :], x2[0:n, t % 2, :]).then_inc(x2_out[t % 2], 16)
                sp.wait_ge(h2_ready, after(t + 1))
                sp.dma_start(h2_d[t0:t0 + n, :], h2[0:n, t % 2, :]).then_inc(h2_out[t % 2], 16)

            for t in range(NTT):
                src, n = x_rows(t)
                if t >= 2:
                    sp.wait_ge(x2_ready, after(t - 1))
                sp.dma_start(x[0:n, t % 2, :], src).then_inc(x_in[t % 2], 16)
                if t >= 1:
                    store(t - 1)
            store(NT)
            for i in range(2):
                sp.wait_ge(x2_out[i], landed((NTT + 1 - i) // 2))
                sp.wait_ge(h2_out[i], landed((NTT + 1 - i) // 2))

        @block.gpsimd
        def _(pool):
            nc.gpsimd.memset(gl[:, :], -3e38).then_inc(ready, 1)
            nc.gpsimd.memset(ones_b[:, :], 1.0).then_inc(ready, 1)
            nc.gpsimd.tensor_copy(tri_b[:, :], consts["tri"]).then_inc(ready, 1)
            nc.gpsimd.memset(m_all[:, :], 0.0).then_inc(ready, 1)
            nc.gpsimd.memset(eid[:, :, :], 0.0).then_inc(ready, 1)
            nc.gpsimd.memset(pos[:, :, :], 0.0).then_inc(ready, 1)

        @block.scalar
        def _(act):
            nc.scalar.preload_act_table_set("natural_log_exp_and_others")
            for k in range(KD):
                act.wait_ge(w_in[k % 4], landed(k // 4 + 1))
                nc.scalar.activation(w_hi[:, k, :], w[:, k % 4, :], ACT.Copy).then_inc(w_hi_done, 1)
            def statistic(t):
                n = TILES[t][1]
                q = stat[0:n, t % 2]
                act.wait_ge(x2_ready, after(t + 1))
                if t >= 2:
                    act.wait_ge(h2_ready, after(t - 1))
                    act.wait_ge(h2_turned, after(t - 1))
                    act.wait_ge(h2_out[t % 2], landed(t // 2))
                nc.scalar.activation(h2[0:n, t % 2, :], x2[0:n, t % 2, :], ACT.Square, scale=float(D) ** -0.5,
                                     accum_out=q[:, 0:1]).then_inc(sumsq, 1)
                act.wait_ge(sumsq, after(t + 1))
                nc.scalar.activation(q[:, 1:2], q[:, 0:1], ACT.Ln, bias=consts["eps"][0:n, :]).then_inc(rstd_act, 1)
                act.wait_ge(rstd_act, after(2 * t + 1))
                nc.scalar.activation(q[:, 2:3], q[:, 1:2], ACT.Exp, scale=-0.5).then_inc(rstd_act, 1)

            def keep_turned(t):
                n = TILES[t][1]
                act.wait_ge(h2_turned, after(t + 1))
                if t:
                    act.wait_ge(logits_done, after(t))
                nc.scalar.activation(hT[:, :, 0:n], p_h[:, :, 0:n], ACT.Copy).then_inc(hT_ready, 1)

            def soft(t):
                n = TILES[t][1]
                act.wait_ge(gmax_ready, after(t + 1))
                nc.scalar.activation(junk[0:n, 0:4], gl[0:n, 0:4], ACT.Exp, bias=f[0:n, 1:2], accum_out=f[0:n, 2:3]).then_inc(gsum_ready, 1)
                act.wait_ge(diff_ready, after(t + 1))
                nc.scalar.activation(f[0:n, 8:9], f[0:n, 7:8], ACT.Exp).then_inc(ratio_ready, 1)

            for t in range(NTT):
                statistic(t)
                if t:
                    soft(t - 1)
                keep_turned(t)
            soft(NT)

        @block.vector
        def _(dve):
            V = nc.vector
            steps = 0

            def step(ins):
                nonlocal steps
                ins.then_inc(routed, 1)
                steps += 1
                dve.wait_ge(routed, after(steps))

            def residual(t):
                n, g = TILES[t][1], int(t == NT)
                dve.wait_ge(m_done, after(t + 1))
                if t >= 2:
                    dve.wait_ge(x2_out[t % 2], landed(t // 2))
                V.tensor_tensor(x2[0:n, t % 2, :], p_m[0:n, t % 2, :], rows[0:n, g, 0, :], ALU.mult).then_inc(m_gated, 1)
                dve.wait_ge(m_gated, after(t + 1))
                dve.wait_ge(x_in[t % 2], landed(t // 2 + 1))
                V.tensor_tensor(x2[0:n, t % 2, :], x2[0:n, t % 2, :], x[0:n, t % 2, :], ALU.add).then_inc(x2_ready, 1)

            def norm(t):
                n, g = TILES[t][1], int(t == NT)
                q = stat[0:n, t % 2]
                dve.wait_ge(rstd_act, after(2 * t + 2))
                rstd_newton(V, dve, q, rstd_dve, 3 * t)
                V.scalar_tensor_tensor(out=h2[0:n, t % 2, :], in0=x2[0:n, t % 2, :], scalar=q[:, 5:6], in1=rows[0:n, g, 1, :],
                                       op0=ALU.mult, op1=ALU.mult).then_inc(h2_scaled, 1)
                dve.wait_ge(h2_scaled, after(t + 1))
                V.tensor_tensor(h2[0:n, t % 2, :], h2[0:n, t % 2, :], rows[0:n, g, 2, :], ALU.add).then_inc(h2_ready, 1)

            def choose(t):
                n = TILES[t][1]
                count = consts["count"][0:n, :]
                group, neg_max, idx, g8, diff = f[0:n, 0:1], f[0:n, 1:2], f[0:n, 4:6], f[0:n, 6:7], f[0:n, 7:8]
                dve.wait_ge(logits_done, after(t + 1))
                step(V.tensor_tensor(gl[0:n, 0:4], p_l[0:n, 0:4], b_r[0:n, 0:4], ALU.add))
                step(V.tensor_tensor(le[0:n].rearrange("p g e -> p (g e)"), p_l[0:n, 4:36], b_r[0:n, 4:36], ALU.add))
                step(V.max(top[0:n, :], gl[0:n, :]))
                V.tensor_scalar(neg_max, top[0:n, 0:1], -1.0, None, ALU.mult).then_inc(gmax_ready, 1)
                step(V.max_index(top_i[0:n, :], top[0:n, :], gl[0:n, :]))
                step(V.tensor_copy(group, top_i[0:n, 0:1]))
                step(V.tensor_scalar(one_g[0:n, :], count[:, 0:4], group, None, ALU.is_equal))
                step(V.tensor_tensor(picked[0:n], le[0:n], one_g[0:n, :].unsqueeze(2).broadcast_to([n, 4, 8]), ALU.mult))
                step(V.tensor_reduce(sel[0:n, :], picked[0:n].rearrange("p g e -> p e g"), AX.X, ALU.add))
                step(V.max(sub_top[0:n, :], sel[0:n, :]))
                V.tensor_tensor(diff, sub_top[0:n, 1:2], sub_top[0:n, 0:1], ALU.subtract).then_inc(diff_ready, 1)
                step(V.max_index(sub_i[0:n, :], sub_top[0:n, :], sel[0:n, :]))
                step(V.tensor_scalar(g8, group, 8.0, None, ALU.mult))
                step(V.tensor_copy(idx, sub_i[0:n, 0:2]))
                step(V.tensor_scalar(eid[0:n, t, :], idx, g8, None, ALU.add))
                step(V.tensor_tensor(hot[0:n], count.unsqueeze(1).broadcast_to([n, 2, 32]),
                                     eid[0:n, t, :].unsqueeze(2).broadcast_to([n, 2, 32]), ALU.is_equal))
                if t:
                    dve.wait_ge(rank_done, after(t))
                    dve.wait_ge(m_all_ready, after(t))
                V.tensor_tensor(m_tile[0:n, :], hot[0:n, 0, :], hot[0:n, 1, :], ALU.add).then_inc(hot_ready, 1)

            def weigh(t):
                n = TILES[t][1]
                gsum, ratio, den = f[0:n, 2:3], f[0:n, 8:9], f[0:n, 9:10]
                dve.wait_ge(gsum_ready, after(t + 1))
                dve.wait_ge(ratio_ready, after(t + 1))
                step(V.scalar_tensor_tensor(out=den, in0=ratio, scalar=1.0, in1=gsum, op0=ALU.add, op1=ALU.mult))
                step(V.reciprocal(wts[0:n, t, 0:1], den))
                step(V.tensor_tensor(wts[0:n, t, 1:2], wts[0:n, t, 0:1], ratio, ALU.mult))
                dve.wait_ge(rank_done, after(t + 1))
                step(V.tensor_tensor(ranked[0:n], hot[0:n], p_r[0:n, 0:32].unsqueeze(1).broadcast_to([n, 2, 32]), ALU.mult))
                step(V.tensor_reduce(pos[0:n, t, :], ranked[0:n], AX.X, ALU.add))
                V.tensor_tensor(m_all[0:n, :], m_all[0:n, :], m_tile[0:n, :], ALU.add).then_inc(m_all_ready, 1)

            for k in range(KD):
                dve.wait_ge(w_hi_done, after(k + 1))
                V.tensor_tensor(w_lo[:, k, :], w[:, k % 4, :], w_hi[:, k, :].bitcast(F32), ALU.subtract).then_inc(w_lo_done, 1)
            dve.wait_ge(rows_in, landed(7))
            for g in range(2):
                V.scalar_tensor_tensor(out=rows[:, g, 1, :], in0=rows[:, g, 1, :], scalar=1.0, in1=x2[:, 0, :],
                                       op0=ALU.add, op1=ALU.mult).then_inc(rows_scaled, 1)
            dve.wait_ge(rows_scaled, after(2))
            dve.wait_ge(small_in, landed(4))
            dve.wait_ge(ready, after(6))
            for t in range(NTT):
                residual(t)
                norm(t)
                if t:
                    choose(t - 1)
                    weigh(t - 1)
            choose(NT)
            weigh(NT)

        @block.tensor
        def _(pe):
            def project(t):
                t0, n = TILES[t]
                if t >= 2:
                    pe.wait_ge(m_gated, after(t - 1))
                for c in range(0, D, 512):
                    for k in range(KD):
                        if t == 0 and c == 0:
                            pe.wait_ge(w_lo_done, after(k + 1))
                        m = split_matmul(nc, p_m[0:n, t % 2, c:c + 512], (m_hi[:, k, t0:t0 + n], m_lo[:, k, t0:t0 + n]),
                                         (w_hi[:, k, c:c + 512], w_lo[:, k, c:c + 512]), k == 0, k == KD - 1)
                m.then_inc(m_done, 1)

            def logits(t):
                n = TILES[t][1]
                pe.wait_ge(h2_ready, after(t + 1))
                if t:
                    pe.wait_ge(hT_ready, after(t))
                for k in range(KD):
                    m = nc.tensor.transpose(p_h[:, k, 0:n], h2[0:n, t % 2, k * P:(k + 1) * P], ident[0:n, 0:n])
                m.then_inc(h2_turned, 1)
                pe.wait_ge(hT_ready, after(t + 1))
                if t:
                    pe.wait_ge(hot_ready, after(t))
                else:
                    pe.wait_ge(small_in, landed(4))
                for k in range(KD):
                    m = nc.tensor.matmul(p_l[0:n, 0:36], hT[:, k, 0:n], w_r[:, k, :], start=(k == 0), stop=(k == KD - 1))
                m.then_inc(logits_done, 1)

            def rank(t):
                n = TILES[t][1]
                pe.wait_ge(hot_ready, after(t + 1))
                if t:
                    pe.wait_ge(m_all_ready, after(t))
                else:
                    pe.wait_ge(ready, after(6))
                nc.tensor.matmul(p_r[0:n, 0:32], tri_b[0:n, 0:n], m_tile[0:n, :], start=True, stop=False)
                nc.tensor.matmul(p_r[0:n, 0:32], ones_b[:, 0:n], m_all[:, :], start=False, stop=True).then_inc(rank_done, 1)

            project(0)
            for t in range(NTT):
                if t + 1 < NTT:
                    project(t + 1)
                if t:
                    rank(t - 1)
                logits(t)
            rank(NT)


NE = 32
F = 512
CAP = 112
NOVER = 2 * T // (CAP + 1)
NSLOT = NE * CAP + NOVER * P
EMPTY = 8192


def weight_buffers(s, B):
    return {"stage": s, "w": (s.sb("w_g", [P, B, KD, F]), s.sb("w_u", [P, B, KD, F]), s.sb("w_d", [P, B, F // P, D])),
            "in": [[s.sem(f"{x}{i}") for i in range(B)] for x in ("g_in", "u_in", "d_in")]}


def expert_parts(a, buffers):
    views = (a["w_e_gate"][0].rearrange("e (k p) f -> p e k f", p=P),
             a["w_e_up"][0].rearrange("e (k p) f -> p e k f", p=P),
             a["w_e_down"][0].rearrange("e (k p) d -> p e k d", p=P))
    return list(zip(buffers["w"], views, buffers["in"]))


def dispatch(nc, a, consts, route, table_d, early):
    NTT = NT + 1
    NK = 2 * NTT
    eid, pos = (route[x][:, :, :].rearrange("p t k -> p (t k)") for x in ("eid", "pos"))
    with Stage(nc, "d") as s:
        ones_b = s.sb("ones_b", [P, P], BF16)
        empty = s.sb("empty", [P, -(-NSLOT // P)], I32)
        value = s.sb("value", [P, NTT, 2], I32)
        cnt, extra, incl, excl, ones = (s.sb(x, [P, NE]) for x in ("cnt", "extra", "incl", "excl", "ones"))
        hot = s.sb("hot", [P, NK, NE])
        first, base, slot, over = (s.sb(x, [P, NK]) for x in ("first", "base", "slot", "over"))
        dest = s.sb("dest", [P, NK], I32)
        before, owner = s.sb("before", [1, NOVER, NE]), s.sb("owner", [1, NOVER])
        p_c = s.psum("c", [P, 512])
        filled, counted, placed, slots_ready, emptied, tabled = (
            s.sem("filled"), s.sem("counted"), s.sem("placed"), s.sem("slots_ready"), s.sem("emptied"), s.soft_sem("tabled"))
        block = s.block()
        whole = NSLOT // P * P

        @block.sync
        def _(sp):
            raise_to_start(sp, s)
            raise_to_start(sp, early["stage"])
            for w, view, sem in expert_parts(a, early):
                sp.dma_start(w[:, 0], view[:, 0]).then_inc(sem[0], 16)

        @block.scalar
        def _(act):
            act.wait_ge(filled, after(3))
            act.dma_start(table_d[0:whole, :].rearrange("(p c) o -> p (c o)", p=P), empty[:, 0:whole // P]).then_inc(emptied, 16)
            if whole < NSLOT:
                act.dma_start(table_d[whole:NSLOT, :].rearrange("(p c) o -> p (c o)", c=1), empty[0:NSLOT - whole, 0:1]).then_inc(emptied, 16)
            act.wait_ge(emptied, landed(1 + (whole < NSLOT)))

        @block.gpsimd
        def _(pool):
            nc.gpsimd.memset(empty[:, :], EMPTY).then_inc(filled, 1)
            nc.gpsimd.memset(ones_b[:, :], 1.0).then_inc(filled, 1)
            nc.gpsimd.memset(ones[:, :], 1.0).then_inc(filled, 1)
            nc.gpsimd.iota(value[:, :, :], pattern=[[2 * P, NTT], [1, 2]], base=0, channel_multiplier=2).then_inc(filled, 1)
            pool.wait_ge(filled, after(4))
            pool.wait_ge(slots_ready, after(1))
            pool.wait_ge(emptied, landed(1 + (whole < NSLOT)))
            for c in range(NK):
                n = TILES[c // 2][1]
                nc.gpsimd.indirect_dma_start(out=table_d, out_offset=bass.IndirectOffsetOnAxis(ap=dest[0:n, c:c + 1], axis=0),
                                             in_=value[0:n, c // 2, c % 2:c % 2 + 1], in_offset=None,
                                             bounds_check=NSLOT - 1, oob_is_err=False).then_inc(tabled, 16)
            pool.wait_ge(tabled, NK * 16)

        @block.vector
        def _(dve):
            V = nc.vector
            steps = 0

            def step(ins):
                nonlocal steps
                ins.then_inc(placed, 1)
                steps += 1
                dve.wait_ge(placed, after(steps))

            def experts_of(x):
                return x.unsqueeze(2).broadcast_to([P, NK, NE])

            dve.wait_ge(counted, after(1))
            dve.wait_ge(filled, after(3))
            step(V.tensor_copy(cnt[:, :], p_c[:, 0:NE]))
            step(V.tensor_scalar(extra[:, :], cnt[:, :], float(CAP), None, ALU.is_gt))
            for lim in range(CAP + P, T, P):
                step(V.scalar_tensor_tensor(out=extra[:, :], in0=cnt[:, :], scalar=float(lim), in1=extra[:, :],
                                            op0=ALU.is_gt, op1=ALU.add))
            step(V.tensor_tensor_scan(incl[:, :], ones[:, :], extra[:, :], 0.0, ALU.mult, ALU.add))
            step(V.tensor_tensor(excl[:, :], incl[:, :], extra[:, :], ALU.subtract))
            step(V.tensor_tensor(hot[:, :, :], consts["count"].unsqueeze(1).broadcast_to([P, NK, NE]), experts_of(eid), ALU.is_equal))
            step(V.tensor_tensor(hot[:, :, :], hot[:, :, :], excl[:, :].unsqueeze(1).broadcast_to([P, NK, NE]), ALU.mult))
            step(V.tensor_reduce(first[:, :], hot[:, :, :], AX.X, ALU.add))
            step(V.scalar_tensor_tensor(out=base[:, :], in0=eid, scalar=float(CAP), in1=pos, op0=ALU.mult, op1=ALU.add))
            step(V.scalar_tensor_tensor(out=slot[:, :], in0=first[:, :], scalar=float(P), in1=pos, op0=ALU.mult, op1=ALU.add))
            step(V.scalar_tensor_tensor(out=slot[:, :], in0=slot[:, :], scalar=float(NE * CAP - CAP), in1=base[:, :],
                                        op0=ALU.add, op1=ALU.subtract))
            step(V.tensor_scalar(over[:, :], pos, float(CAP), None, ALU.is_ge))
            step(V.tensor_tensor(slot[:, :], slot[:, :], over[:, :], ALU.mult))
            step(V.tensor_tensor(slot[:, :], slot[:, :], base[:, :], ALU.add))
            V.tensor_copy(dest[:, :], slot[:, :]).then_inc(slots_ready, 1)
            step(V.tensor_tensor(before[:, :, :], incl[0:1, :].unsqueeze(1).broadcast_to([1, NOVER, NE]),
                                 consts["count"][0:1, 0:NOVER].unsqueeze(2).broadcast_to([1, NOVER, NE]), ALU.is_le))
            step(V.tensor_reduce(owner[:, :], before[:, :, :], AX.X, ALU.add))
            step(V.tensor_scalar(owner[:, :], owner[:, :], float(NE - 1), None, ALU.min))
            step(V.tensor_copy(route["owner"][0:1, 0:NOVER], owner[:, :]))
            step(V.tensor_copy(route["n_extra"][0:1, 0:1], incl[0:1, NE - 1:NE]))

        @block.tensor
        def _(pe):
            pe.wait_ge(filled, after(3))
            nc.tensor.matmul(p_c[:, 0:NE], ones_b[:, :], route["m_all"][:, :], start=True, stop=True).then_inc(counted, 1)


def experts(nc, a, route, table_d, h2_d, y_d, ident, name, N, FIRST, COUNT, early):
    KF = F // P
    with Stage(nc, name) as s:
        dynamic = early is None
        B = 1 if dynamic else 2
        buffers = early or weight_buffers(s, B)
        (w_g, w_u, w_d), (g_in, u_in, d_in) = buffers["w"], buffers["in"]
        tbl, src = s.sb("tbl", [N, COUNT], I32), s.sb("src", [N, COUNT], I32)
        gi, yi, first_load = s.sb("gi", [N, B], I32), s.sb("yi", [N, B], I32), s.sb("first_load", [1, 2 * B], I32)
        xg, xT = s.sb("xg", [N, B, D]), s.sb("xT", [P, B, KD, N])
        act_t, y = s.sb("act_t", [P, B, KF * N]), s.sb("y", [N, B, D])
        hid_hi, hid_lo = s.sb("hid_hi", [P, B, KF, N], F32R), s.sb("hid_lo", [P, B, KF, N], F32R)
        w_d_hi, w_d_lo = s.sb("w_d_hi", [P, KF, D], F32R), s.sb("w_d_lo", [P, KF, D], F32R)
        w_d_hi_done, w_d_lo_done, hid_step = s.sem("w_d_hi_done"), s.sem("w_d_lo_done"), s.sem("hid_step")
        p_x, p_y = s.psum("x", [P, 2, 512]), s.psum("y", [P, D])
        p_g, p_u = s.psum("g", [P, B, 512]), s.psum("u", [P, B, 512])
        tbl_in, src_ready, cleared = s.sem("tbl_in"), s.sem("src_ready"), s.sem("cleared")
        x_in, y_out = ([s.soft_sem(f"{x}{i}") for i in range(B)] for x in ("x_in", "y_out"))
        gi_ready, yi_ready, x_turned, xT_ready = s.sem("gi_ready"), s.sem("yi_ready"), s.sem("x_turned"), s.sem("xT_ready")
        g_done, u_done, silu_act, silu_dve, hid_ready, y_done, y_kept = (
            s.sem("g_done"), s.sem("u_done"), s.sem("silu_act"), s.sem("silu_dve"), s.sem("hid_ready"), s.sem("y_done"),
            s.sem("y_kept"))
        block = s.block()
        def number(eng):
            return eng.value_load(route["n_extra"][0:1, 0:1], min_val=0, max_val=COUNT)

        @block.sync
        def _(sp):
            raise_to_start(sp, s)
            sp.dma_start(tbl[:, :], table_d[FIRST:FIRST + N * COUNT, :].rearrange("(e p) o -> p (e o)", p=N),
                         allow_slow_non_contiguous=True).then_inc(tbl_in, 16)

            def load(e, b, who):
                for (dst, view, sem), free in zip(expert_parts(a, buffers), (g_done, u_done, w_d_lo_done)):
                    sp.wait_ge(free, after(e - B + 1))
                    if not isinstance(e, int):
                        hold(sp, s)
                    sp.dma_start(dst[:, b], view[:, bass.ds(who, 1)].rearrange("p e k f -> p (e k) f")).then_inc(sem[b], 16)

            if dynamic:
                n = number(sp)
                with sp.If(n > 0):
                    with sp.Fori(0, n) as e:
                        load(e, 0, sp.value_load(route["owner"][0:1, bass.ds(e, 1)], min_val=0, max_val=NE - 1))
            else:
                sp.wait_ge(x_in[1], arrived(1))
                load(1, 1, 1)
                with sp.Fori(1, COUNT // 2) as i:
                    for b in range(2):
                        who = sp.snap(i * 2 + b)
                        load(i * 2 + b, b, who)

        @block.gpsimd
        def _(pool):
            for b in range(B):
                pool.dma_start(first_load[0:1, 2 * b:2 * b + 1], table_d[FIRST:FIRST + 1, :]).then_inc(x_in[b], 16)
                pool.dma_start(first_load[0:1, 2 * b + 1:2 * b + 2], table_d[FIRST:FIRST + 1, :]).then_inc(y_out[b], 16)
            nc.gpsimd.memset(xg[:, :, :], 0.0).then_inc(cleared, 1)

            def gather(e, b, u):
                reg = not isinstance(e, int)
                pool.wait_ge(x_in[b], arrived(u))
                if reg:
                    hold(pool, s)
                nc.gpsimd.tensor_copy(gi[:, b:b + 1], src[:, bass.ds(e, 1)]).then_inc(gi_ready, 1)
                pool.wait_ge(gi_ready, after(e + 1))
                pool.wait_ge(x_turned, after(e - B + 1))
                if reg:
                    hold(pool, s)
                nc.gpsimd.indirect_dma_start(out=xg[:, b, :], out_offset=None, in_=h2_d,
                                             in_offset=bass.IndirectOffsetOnAxis(ap=gi[:, b:b + 1], axis=0),
                                             bounds_check=T - 1, oob_is_err=False).then_inc(x_in[b], 16)

            def scatter(e, b, u):
                reg = not isinstance(e, int)
                pool.wait_ge(y_out[b], arrived(u))
                if reg:
                    hold(pool, s)
                nc.gpsimd.tensor_copy(yi[:, b:b + 1], tbl[:, bass.ds(e, 1)]).then_inc(yi_ready, 1)
                pool.wait_ge(yi_ready, after(e + 1))
                pool.wait_ge(y_kept, after(e + 1))
                if reg:
                    hold(pool, s)
                nc.gpsimd.indirect_dma_start(out=y_d, out_offset=bass.IndirectOffsetOnAxis(ap=yi[:, b:b + 1], axis=0),
                                             in_=y[:, b, :], in_offset=None,
                                             bounds_check=2 * T - 1, oob_is_err=False).then_inc(y_out[b], 16)

            pool.wait_ge(cleared, after(1))
            pool.wait_ge(src_ready, after(1))
            if dynamic:
                n = number(pool)
                with pool.If(n > 0):
                    with pool.Fori(0, n) as e:
                        gather(e, 0, e)
                        scatter(e, 0, e)
                pool.wait_ge(y_out[0], arrived(n))
            else:
                gather(0, 0, 0)
                gather(1, 1, 0)
                gather(2, 0, 1)
                with pool.Fori(0, COUNT // 2 - 2) as i:
                    gather(i * 2 + 3, 1, i + 1)
                    scatter(i * 2, 0, i)
                    gather(i * 2 + 4, 0, i + 2)
                    scatter(i * 2 + 1, 1, i)
                gather(COUNT - 1, 1, COUNT // 2 - 1)
                for e in range(COUNT - 4, COUNT):
                    scatter(e, e % 2, e // 2)
                for b in range(2):
                    pool.wait_ge(y_out[b], arrived(COUNT // 2))

        @block.scalar
        def _(act):
            nc.scalar.preload_act_table_set("natural_log_exp_and_others")

            def keep_x(e, b):
                act.wait_ge(x_turned, after(e + 1))
                act.wait_ge(u_done, after(e - B + 1))
                nc.scalar.activation(xT[:, b].rearrange("p (a k) n -> p a (k n)", a=2), p_x[:, :, 0:4 * N], ACT.Copy).then_inc(xT_ready, 1)

            def silu(e, b):
                t = act_t[:, b, :]
                act.wait_ge(g_done, after(e + 1))
                act.wait_ge(hid_ready, after(e - B + 1))
                nc.scalar.activation(t, p_g[:, b, 0:KF * N], ACT.Abs).then_inc(silu_act, 1)
                act.wait_ge(silu_act, after(e * 4 + 1))
                nc.scalar.activation(t, t, ACT.Exp, scale=-1.0).then_inc(silu_act, 1)
                act.wait_ge(silu_act, after(e * 4 + 2))
                nc.scalar.activation(t, t, ACT.Ln, bias=1.0).then_inc(silu_act, 1)
                act.wait_ge(silu_dve, after(e * 2 + 1))
                nc.scalar.activation(t, t, ACT.Exp).then_inc(silu_act, 1)

            def split_down(e, b, u):
                act.wait_ge(d_in[b], landed(u + 1))
                act.wait_ge(y_done, after(e))
                nc.scalar.activation(w_d_hi[:, :, :], w_d[:, b], ACT.Copy).then_inc(w_d_hi_done, 1)

            def keep_y(e, b, u):
                act.wait_ge(y_done, after(e + 1))
                act.wait_ge(y_out[b], arrived(u))
                nc.scalar.activation(y[:, b, :], p_y[0:N, :], ACT.Copy).then_inc(y_kept, 1)

            if dynamic:
                n = number(act)
                with act.If(n > 0):
                    with act.Fori(0, n) as e:
                        keep_x(e, 0)
                        silu(e, 0)
                        split_down(e, 0, e)
                        keep_y(e, 0, e)
            else:
                keep_x(0, 0)
                silu(0, 0)
                keep_x(1, 1)
                split_down(0, 0, 0)
                with act.Fori(0, COUNT // 2 - 1) as i:
                    silu(i * 2 + 1, 1)
                    keep_x(i * 2 + 2, 0)
                    keep_y(i * 2, 0, i)
                    split_down(i * 2 + 1, 1, i)
                    silu(i * 2 + 2, 0)
                    keep_x(i * 2 + 3, 1)
                    keep_y(i * 2 + 1, 1, i)
                    split_down(i * 2 + 2, 0, i + 1)
                silu(COUNT - 1, 1)
                keep_y(COUNT - 2, 0, COUNT // 2 - 1)
                split_down(COUNT - 1, 1, COUNT // 2 - 1)
                keep_y(COUNT - 1, 1, COUNT // 2 - 1)

        @block.vector
        def _(dve):
            V = nc.vector
            dve.wait_ge(tbl_in, landed(1))
            V.tensor_scalar(src[:, :], tbl[:, :], 1, None, ALU.logical_shift_right).then_inc(src_ready, 1)

            def hidden(e, b):
                t = act_t[:, b, :]
                dve.wait_ge(silu_act, after(e * 4 + 3))
                V.scalar_tensor_tensor(out=t, in0=p_g[:, b, 0:KF * N], scalar=0.0, in1=t, op0=ALU.min, op1=ALU.subtract).then_inc(silu_dve, 1)
                dve.wait_ge(silu_act, after(e * 4 + 4))
                V.tensor_tensor(t, t, p_g[:, b, 0:KF * N], ALU.mult).then_inc(silu_dve, 1)
                dve.wait_ge(silu_dve, after(e * 2 + 2))
                dve.wait_ge(u_done, after(e + 1))
                dve.wait_ge(y_done, after(e - B + 1))
                V.tensor_tensor(t, t, p_u[:, b, 0:KF * N], ALU.mult).then_inc(hid_step, 1)
                dve.wait_ge(hid_step, after(e * 2 + 1))
                hi, lo = (x[:, b].rearrange("p k n -> p (k n)") for x in (hid_hi, hid_lo))
                V.tensor_copy(hi, t).then_inc(hid_step, 1)
                dve.wait_ge(hid_step, after(e * 2 + 2))
                V.tensor_tensor(lo, t, hi.bitcast(F32), ALU.subtract).then_inc(hid_ready, 1)
                dve.wait_ge(w_d_hi_done, after(e + 1))
                V.tensor_tensor(w_d_lo[:, :, :], w_d[:, b], w_d_hi[:, :, :].bitcast(F32), ALU.subtract).then_inc(w_d_lo_done, 1)

            if dynamic:
                n = number(dve)
                with dve.If(n > 0):
                    with dve.Fori(0, n) as e:
                        hidden(e, 0)
            else:
                with dve.Fori(0, COUNT // 2) as i:
                    hidden(i * 2, 0)
                    hidden(i * 2 + 1, 1)

        @block.tensor
        def _(pe):
            def turn(e, b, u):
                pe.wait_ge(x_in[b], arrived(u + 1))
                pe.wait_ge(xT_ready, after(e))
                if not isinstance(e, int):
                    hold(pe, s)
                for k in range(KD):
                    m = nc.tensor.transpose(p_x[:, k // 4, (k % 4) * N:(k % 4 + 1) * N], xg[:, b, k * P:(k + 1) * P], ident[0:N, 0:N])
                m.then_inc(x_turned, 1)

            def gate_up(e, b, u):
                pe.wait_ge(xT_ready, after(e + 1))
                for w, p, into, done in ((w_g, p_g, g_in, g_done), (w_u, p_u, u_in, u_done)):
                    pe.wait_ge(into[b], landed(u + 1))
                    pe.wait_ge(hid_ready, after(e - B + 1))
                    for f in range(KF):
                        for k in range(KD):
                            m = nc.tensor.matmul(p[:, b, f * N:(f + 1) * N], w[:, b, k, f * P:(f + 1) * P], xT[:, b, k, :],
                                                 start=(k == 0), stop=(k == KD - 1))
                    m.then_inc(done, 1)

            def down(e, b, u):
                pe.wait_ge(hid_ready, after(e + 1))
                pe.wait_ge(w_d_lo_done, after(e + 1))
                pe.wait_ge(y_kept, after(e))
                if not isinstance(e, int):
                    hold(pe, s)
                for c in range(0, D, 512):
                    for f in range(KF):
                        m = split_matmul(nc, p_y[0:N, c:c + 512], (hid_hi[:, b, f, :], hid_lo[:, b, f, :]),
                                         (w_d_hi[:, f, c:c + 512], w_d_lo[:, f, c:c + 512]), f == 0, f == KF - 1)
                m.then_inc(y_done, 1)

            pe.wait_ge(cleared, after(1))
            if dynamic:
                n = number(pe)
                with pe.If(n > 0):
                    with pe.Fori(0, n) as e:
                        turn(e, 0, e)
                        gate_up(e, 0, e)
                        down(e, 0, e)
            else:
                turn(0, 0, 0)
                gate_up(0, 0, 0)
                turn(1, 1, 0)
                with pe.Fori(0, COUNT // 2 - 1) as i:
                    gate_up(i * 2 + 1, 1, i)
                    turn(i * 2 + 2, 0, i + 1)
                    down(i * 2, 0, i)
                    gate_up(i * 2 + 2, 0, i + 1)
                    turn(i * 2 + 3, 1, i + 1)
                    down(i * 2 + 1, 1, i)
                gate_up(COUNT - 1, 1, COUNT // 2 - 1)
                down(COUNT - 2, 0, COUNT // 2 - 1)
                down(COUNT - 1, 1, COUNT // 2 - 1)


def combine(nc, a, mod_d, x2_d, y_d, outs, consts, route):
    NTT = NT + 1
    wts = route["wts"]
    with Stage(nc, "z") as s:
        g2, nf = s.sb("g2", [P, 2, D]), s.sb("nf", [P, D])
        y, x2 = s.sb("y", [P, 4, 2, D]), s.sb("x2", [P, 4, D])
        y1, x3, out, junk = s.sb("y1", [P, 3, D]), s.sb("x3", [P, 2, D]), s.sb("out", [P, 2, D]), s.sb("junk", [P, D])
        stat = s.sb("stat", [P, 2, 8])
        rows_in = s.sem("rows_in")
        y_in, x2_in = [s.sem(f"y_in{i}") for i in range(4)], [s.sem(f"x2_in{i}") for i in range(4)]
        out_done = [s.sem(f"out_done{i}") for i in range(2)]
        y_scaled, y_summed, y_gated, x3_ready, sumsq, rstd_act, rstd_dve, out_ready = (
            s.sem("y_scaled"), s.sem("y_summed"), s.sem("y_gated"), s.sem("x3_ready"), s.sem("sumsq"), s.sem("rstd_act"),
            s.sem("rstd_dve"), s.sem("out_ready"))
        block = s.block()
        y_rows = y_d.rearrange("(t k) d -> t k d", k=2)

        @block.sync
        def _(sp):
            raise_to_start(sp, s)
            for g in range(2):
                sp.dma_start(g2[:, g, :], mod_d[g:g + 1, 5 * D:6 * D].partition_broadcast(P)).then_inc(rows_in, 16)
            sp.dma_start(nf[:, :], a["norm_final"].rearrange("(o d) -> o d", o=1).partition_broadcast(P)).then_inc(rows_in, 16)

            def load(t):
                t0, n = TILES[t]
                if t >= 4:
                    sp.wait_ge(x3_ready, after(t - 3))
                sp.dma_start(y[0:n, t % 4], y_rows[t0:t0 + n]).then_inc(y_in[t % 4], 16)
                sp.dma_start(x2[0:n, t % 4, :], x2_d[t0:t0 + n, :]).then_inc(x2_in[t % 4], 16)

            for t in range(4):
                load(t)
            for t in range(NTT):
                t0, n = TILES[t]
                dst = outs[0][0, t0:t0 + n, :] if t < NT else outs[1][0]
                sp.wait_ge(out_ready, after(t + 1))
                sp.dma_start(dst, out[0:n, t % 2, :]).then_inc(out_done[t % 2], 16)
                if t + 4 < NTT:
                    load(t + 4)
            for i in range(2):
                sp.wait_ge(out_done[i], landed((NTT + 1 - i) // 2))

        @block.gpsimd
        def _(pool):
            for t in range(NTT):
                t0, n = TILES[t]
                pool.wait_ge(y_gated, after(t + 1))
                pool.wait_ge(x2_in[t % 4], landed(t // 4 + 1))
                if t >= 2:
                    pool.wait_ge(out_ready, after(t - 1))
                nc.gpsimd.tensor_tensor(x3[0:n, t % 2, :], y[0:n, t % 4, 1, :], x2[0:n, t % 4, :], ALU.add).then_inc(x3_ready, 1)

        @block.scalar
        def _(act):
            nc.scalar.preload_act_table_set("natural_log_exp_and_others")

            def scale_y(t):
                n = TILES[t][1]
                act.wait_ge(y_in[t % 4], landed(t // 4 + 1))
                if t >= 3:
                    act.wait_ge(y_summed, after(t - 2))
                nc.scalar.activation(y1[0:n, t % 3, :], y[0:n, t % 4, 0, :], ACT.Copy, scale=wts[0:n, t, 0:1]).then_inc(y_scaled, 1)

            scale_y(0)
            scale_y(1)
            for t in range(NTT):
                n = TILES[t][1]
                if t + 2 < NTT:
                    scale_y(t + 2)
                q = stat[0:n, t % 2]
                act.wait_ge(x3_ready, after(t + 1))
                nc.scalar.activation(junk[0:n, :], x3[0:n, t % 2, :], ACT.Square, scale=float(D) ** -0.5,
                                     accum_out=q[:, 0:1]).then_inc(sumsq, 1)
                act.wait_ge(sumsq, after(t + 1))
                nc.scalar.activation(q[:, 1:2], q[:, 0:1], ACT.Ln, bias=consts["eps"][0:n, :]).then_inc(rstd_act, 1)
                act.wait_ge(rstd_act, after(2 * t + 1))
                nc.scalar.activation(q[:, 2:3], q[:, 1:2], ACT.Exp, scale=-0.5).then_inc(rstd_act, 1)

        @block.vector
        def _(dve):
            V = nc.vector

            def mixed(t):
                n, g = TILES[t][1], int(t == NT)
                yt = y[0:n, t % 4, 1, :]
                dve.wait_ge(y_scaled, after(t + 1))
                V.scalar_tensor_tensor(out=yt, in0=yt, scalar=wts[0:n, t, 1:2], in1=y1[0:n, t % 3, :],
                                       op0=ALU.mult, op1=ALU.add).then_inc(y_summed, 1)
                dve.wait_ge(y_summed, after(t + 1))
                V.tensor_tensor(yt, yt, g2[0:n, g, :], ALU.mult).then_inc(y_gated, 1)

            dve.wait_ge(rows_in, landed(3))
            mixed(0)
            for t in range(NTT):
                n = TILES[t][1]
                if t + 1 < NTT:
                    mixed(t + 1)
                q = stat[0:n, t % 2]
                dve.wait_ge(rstd_act, after(2 * t + 2))
                rstd_newton(V, dve, q, rstd_dve, 3 * t)
                if t >= 2:
                    dve.wait_ge(out_done[t % 2], landed(t // 2))
                V.scalar_tensor_tensor(out=out[0:n, t % 2, :], in0=x3[0:n, t % 2, :], scalar=q[:, 5:6], in1=nf[0:n, :],
                                       op0=ALU.mult, op1=ALU.mult).then_inc(out_ready, 1)


INPUTS = ["x_prompt", "x_sample", "c_prompt", "c_sample", "state_hgrn", "state_gla", "w_ada", "b_ada", "norm_mix",
          "norm_ffn", "w_in", "hg_lb", "hg_onorm", "w_gk2", "b_gk", "gla_onorm", "w_br_a", "w_br_b", "w_out", "w_rg",
          "b_rg", "w_re", "b_re", "w_e_gate", "w_e_up", "w_e_down", "norm_final"]


def shape_constants():
    s, t = np.arange(P)[:, None] % 64, np.arange(64)[None, :]
    levels = [s == t]
    for h in HALVES[1:]:
        levels.append((s // (2 * h) == t // (2 * h)) & (s % (2 * h) < h) & (t % (2 * h) >= h))
    tri = np.arange(P)[:, None] < np.arange(P)[None, :]
    count = np.broadcast_to(np.arange(32), (P, 32))
    return np.concatenate([x.astype(np.float32) for x in levels + [tri, count]], axis=1)


NMASK = NL * 64


def program(nc, a, outs, scratch):
    with Stage(nc, "all") as s:
        ident = s.sb("ident", [P, P])
        ones, mean = s.sb("ones", [P, P]), s.sb("mean", [P, P])
        eps = s.sb("eps", [P, 1])
        onorm = s.sb("onorm", [P, 2])
        shapes = s.sb("shapes", [P, NMASK + P + 32])
        consts = {"ones": ones, "mean": mean, "eps": eps, "onorm_hg": onorm[:, 0:1], "onorm_gla": onorm[:, 1:2],
                  "masks": shapes[:, 0:NMASK].rearrange("p (l t) -> p l t", t=64),
                  "tri": shapes[:, NMASK:NMASK + P], "count": shapes[:, NMASK + P:NMASK + P + NE]}
        NTT = NT + 1
        route = {"eid": s.sb("eid", [P, NTT, 2]), "pos": s.sb("pos", [P, NTT, 2]), "wts": s.sb("wts", [P, NTT, 2]),
                 "m_all": s.sb("m_all", [P, NE], BF16),
                 "owner": s.sb("owner", [1, NOVER], I32), "n_extra": s.sb("n_extra", [1, 1], I32)}
        filled, consts_in = s.sem("filled"), s.sem("consts_in")
        with nc.Block() as block:
            @block.gpsimd
            def _(pool):
                nc.gpsimd.memset(ones[:, :], 1.0).then_inc(filled, 1)
                nc.gpsimd.memset(mean[:, :], 1.0 / P).then_inc(filled, 1)
                nc.gpsimd.memset(eps[:, :], EPS).then_inc(filled, 1)

            @block.sync
            def _(sp):
                sp.dma_start(shapes[:, :], a["shapes"]).then_inc(consts_in, 16)
                sp.dma_start(onorm[:, 0:1], a["hg_onorm"].rearrange("l v -> v l")).then_inc(consts_in, 16)
                sp.dma_start(onorm[:, 1:2], a["gla_onorm"].rearrange("l v -> v l")).then_inc(consts_in, 16)
                sp.wait_ge(filled, 3)
                sp.wait_ge(consts_in, 48)
        with Stage(nc, "h") as h:
            h_hi = h.sb("hi", [P, KD, T], F32R)
            h_lo = h.sb("lo", [P, KD, T], F32R)
            condition(nc, a, scratch["mod"], h_hi, h_lo, ident)
            for kind, o in (("hg", (outs[2], outs[4])), ("gla", (outs[3], outs[5]))):
                rows = tuple(x.rearrange("l b h k v -> (l b h k) v") for x in o)
                mix_heads(nc, a, kind, h_hi, h_lo, ident, scratch["mix"], scratch["gate"], rows, consts)
        with Stage(nc, "mg") as m:
            m_hi, m_lo = m.sb("hi", [P, KD, T], F32R), m.sb("lo", [P, KD, T], F32R)
            merge(nc, a, scratch["mix"], scratch["gate"], m_hi, m_lo)
            out_router(nc, a, scratch["mod"], scratch["x2"], scratch["h2"], m_hi, m_lo, ident, consts, route)
        lists = (scratch["table"], scratch["h2"], scratch["y"], ident)
        with Stage(nc, "ew") as ew:
            early = weight_buffers(ew, 2)
            dispatch(nc, a, consts, route, scratch["table"], early)
            experts(nc, a, route, *lists, "e", CAP, 0, NE, early)
            ew.clear()
        experts(nc, a, route, *lists, "v", P, NE * CAP, NOVER, None)
        combine(nc, a, scratch["mod"], scratch["x2"], scratch["y"], outs, consts, route)


OUTPUTS = [(1, T_PROMPT, D), (1, T_SAMPLE, D), (1, 1, HG_HEADS, HG_DK, DV), (1, 1, GLA_HEADS, GLA_DK, DV),
           (1, 1, HG_HEADS, HG_DK, DV), (1, 1, GLA_HEADS, GLA_DK, DV)]
SCRATCH = {"mod": ((2, 6 * D), F32), "mix": ((8, P, T), F32), "gate": ((16, P, T), F32), "x2": ((T, D), F32), "h2": ((T, D), F32),
           "y": ((2 * T, D), F32), "table": ((NSLOT, 1), I32)}


def kernel(**inputs):
    import concourse.bacc as bacc
    from concourse.bass_utils import run_bass_kernel_spmd as run

    nc = bacc.Bacc("TRN2", target_bir_lowering=False, num_devices=1)
    arrays, a = {}, {}
    for name, x in [(n, inputs[n]) for n in INPUTS] + [("shapes", shape_constants())]:
        x = np.ascontiguousarray(x)
        arrays[f"in_{name}"] = x
        a[name] = nc.dram_tensor(f"in_{name}", x.shape, mybir.dt.from_np(x.dtype), kind="ExternalInput").ap()
    outs = [nc.dram_tensor(f"out_{i}", shape, F32, kind="ExternalOutput").ap() for i, shape in enumerate(OUTPUTS)]
    scratch = {n: nc.dram_tensor(f"scratch_{n}", shape, dtype).ap() for n, (shape, dtype) in SCRATCH.items()}
    program(nc, a, outs, scratch)
    r = run(nc, [arrays], core_ids=[0])
    return tuple(r.results[0][f"out_{i}"] for i in range(len(OUTPUTS)))
```
